# Optimizing a Trainium2 kernel written in Bass

```python
import jax, jax.numpy as jnp
from jax import lax
import numpy as np
import math

D_MODEL = 1024
BATCH = 1
SEQ = 512
DEPTH = 2

CHUNK = 64
LEFT_CHUNKS = 8
BAND_CHUNKS = LEFT_CHUNKS + 1
N_HEADS = 16
HEAD_DIM = D_MODEL // N_HEADS
REL_CLIP = 128
LRU_WIDTH = ((4 * D_MODEL // 3 + 127) // 128) * 128
N_LRU_BLOCKS = 16
LRU_BLOCK = LRU_WIDTH // N_LRU_BLOCKS
LRU_C = 8.0
CONV_WIDTH = 4
D_FF = 4 * D_MODEL
N_A_LAYERS = DEPTH // 2
N_B_LAYERS = DEPTH - N_A_LAYERS
EPS = 1e-6


def rms_norm(x, g):
    xf = x.astype(jnp.float32)
    y = xf * lax.rsqrt(jnp.mean(xf * xf, axis=-1, keepdims=True) + EPS)
    return (y * g.astype(jnp.float32)).astype(x.dtype)

def modulate(x, shift, scale):
    return x * (1 + scale[:, None, :]) + shift[:, None, :]

def causal_depthwise_conv(x, w, b):
    y = lax.conv_general_dilated(
        x, w[:, None, :].astype(x.dtype), window_strides=(1,),
        padding=[(CONV_WIDTH - 1, 0)],
        dimension_numbers=("NWC", "WIO", "NWC"),
        feature_group_count=x.shape[-1])
    return y + b

def rg_lru(x, w_a, b_a, w_x, b_x, lam):
    bsz, s, w = x.shape
    xb = x.reshape(bsz, s, N_LRU_BLOCKS, LRU_BLOCK)
    r = jax.nn.sigmoid(jnp.einsum("bsnd,nde->bsne", xb, w_a).reshape(bsz, s, w) + b_a)
    i = jax.nn.sigmoid(jnp.einsum("bsnd,nde->bsne", xb, w_x).reshape(bsz, s, w) + b_x)
    log_a = (-LRU_C * r.astype(jnp.float32)) * jax.nn.softplus(-lam.astype(jnp.float32))
    a = jnp.exp(log_a)
    mult = jnp.sqrt(-jnp.expm1(2.0 * log_a))
    u = mult * (i * x).astype(jnp.float32)

    def combine(left, right):
        a_l, b_l = left
        a_r, b_r = right
        return a_r * a_l, a_r * b_l + b_r

    _, h = lax.associative_scan(combine, (a, u), axis=1)
    return h.astype(x.dtype)

def recurrent_mixer(hn, w_in, conv_w, conv_b, gate_a_w, gate_a_b, gate_x_w, gate_x_b, lam, w_out):
    z = hn @ w_in
    gate, xr = jnp.split(z, 2, axis=-1)
    xr = causal_depthwise_conv(xr, conv_w, conv_b)
    y = rg_lru(xr, gate_a_w, gate_a_b, gate_x_w, gate_x_b, lam)
    return (y * jax.nn.gelu(gate)) @ w_out

def shared_kv(h, c_act, kv_norm_g, kv_ada_w, kv_ada_b, kv_w, k_norm_g):
    bsz, s, _ = h.shape
    shift, scale = jnp.split(c_act @ kv_ada_w + kv_ada_b, 2, axis=-1)
    hn = modulate(rms_norm(h, kv_norm_g), shift, scale)
    k, v = jnp.split(hn @ kv_w, 2, axis=-1)
    k = rms_norm(k.reshape(bsz, s, N_HEADS, HEAD_DIM), k_norm_g)
    v = v.reshape(bsz, s, N_HEADS, HEAD_DIM)
    pad = ((0, 0), (LEFT_CHUNKS * CHUNK, 0), (0, 0), (0, 0))
    return jnp.pad(k, pad), jnp.pad(v, pad)

def chunk_attention(hn, w_q, q_norm_g, rel_bias, w_o, k_pad, v_pad):
    bsz, s, d = hn.shape
    n_chunks = s // CHUNK
    band = BAND_CHUNKS * CHUNK
    left = LEFT_CHUNKS * CHUNK
    q = rms_norm((hn @ w_q).reshape(bsz, s, N_HEADS, HEAD_DIM), q_norm_g)
    q_chunks = q.reshape(bsz, n_chunks, CHUNK, N_HEADS, HEAD_DIM).transpose(1, 0, 2, 3, 4)
    rel = jnp.arange(CHUNK)[:, None] - (jnp.arange(band)[None, :] - left)
    rel_idx = jnp.clip(rel, -REL_CLIP, REL_CLIP) + REL_CLIP
    bias = rel_bias[:, rel_idx].astype(jnp.float32)
    scale = HEAD_DIM ** -0.5

    def one_chunk(args):
        qc, ci = args
        start = ci * CHUNK
        kc = lax.dynamic_slice_in_dim(k_pad, start, band, axis=1)
        vc = lax.dynamic_slice_in_dim(v_pad, start, band, axis=1)
        sc = jnp.einsum("bqhd,bkhd->bhqk", qc, kc,
                        preferred_element_type=jnp.float32) * scale + bias
        valid = (start - left + jnp.arange(band)) >= 0
        sc = jnp.where(valid[None, None, None, :], sc, -1e30)
        p = jax.nn.softmax(sc, axis=-1).astype(vc.dtype)
        return jnp.einsum("bhqk,bkhd->bqhd", p, vc)

    out = lax.map(one_chunk, (q_chunks, jnp.arange(n_chunks)))
    out = out.transpose(1, 0, 2, 3, 4).reshape(bsz, s, d)
    return out @ w_o

def sqrelu_mlp(hn, w1, w2):
    return jnp.square(jax.nn.relu(hn @ w1)) @ w2

def first_inputs(seed: int = 0) -> dict:
    key = jax.random.key(seed)
    ks = jax.random.split(key, 32)
    f32 = jnp.float32
    D, W = D_MODEL, LRU_WIDTH

    def nrm(k, shape, fan_in):
        return jax.random.normal(k, shape, f32) * (fan_in ** -0.5)

    u = jax.random.uniform(ks[10], (N_A_LAYERS, W), f32, 0.9, 0.999)
    a0 = u ** (1.0 / LRU_C)
    lru_lambda = jnp.log(a0) - jnp.log1p(-a0)
    return {
        "x": jax.random.normal(ks[0], (BATCH, SEQ, D), f32),
        "c": jax.random.normal(ks[1], (BATCH, D), f32),
        "ada_w": nrm(ks[2], (DEPTH, D, 6 * D), D),
        "ada_b": 0.02 * jax.random.normal(ks[3], (DEPTH, 6 * D), f32),
        "norm1_g": 1.0 + 0.05 * jax.random.normal(ks[4], (DEPTH, D), f32),
        "norm2_g": 1.0 + 0.05 * jax.random.normal(ks[5], (DEPTH, D), f32),
        "mlp_w1": nrm(ks[6], (DEPTH, D, D_FF), D),
        "mlp_w2": nrm(ks[7], (DEPTH, D_FF, D), D_FF),
        "lru_w_in": nrm(ks[8], (N_A_LAYERS, D, 2 * W), D),
        "lru_conv_w": nrm(ks[9], (N_A_LAYERS, CONV_WIDTH, W), CONV_WIDTH),
        "lru_conv_b": 0.02 * jax.random.normal(ks[11], (N_A_LAYERS, W), f32),
        "lru_gate_a_w": nrm(ks[12], (N_A_LAYERS, N_LRU_BLOCKS, LRU_BLOCK, LRU_BLOCK), LRU_BLOCK),
        "lru_gate_a_b": 0.02 * jax.random.normal(ks[13], (N_A_LAYERS, W), f32),
        "lru_gate_x_w": nrm(ks[14], (N_A_LAYERS, N_LRU_BLOCKS, LRU_BLOCK, LRU_BLOCK), LRU_BLOCK),
        "lru_gate_x_b": 0.02 * jax.random.normal(ks[15], (N_A_LAYERS, W), f32),
        "lru_lambda": lru_lambda,
        "lru_w_out": nrm(ks[16], (N_A_LAYERS, W, D), W),
        "kv_norm_g": 1.0 + 0.05 * jax.random.normal(ks[17], (D,), f32),
        "kv_ada_w": nrm(ks[18], (D, 2 * D), D),
        "kv_ada_b": 0.02 * jax.random.normal(ks[19], (2 * D,), f32),
        "kv_w": nrm(ks[20], (D, 2 * D), D),
        "k_norm_g": 1.0 + 0.05 * jax.random.normal(ks[21], (HEAD_DIM,), f32),
        "attn_w_q": nrm(ks[22], (N_B_LAYERS, D, D), D),
        "q_norm_g": 1.0 + 0.05 * jax.random.normal(ks[23], (N_B_LAYERS, HEAD_DIM), f32),
        "rel_bias": 0.5 * jax.random.normal(ks[24], (N_B_LAYERS, N_HEADS, 2 * REL_CLIP + 1), f32),
        "attn_w_o": nrm(ks[25], (N_B_LAYERS, D, D), D),
    }

def first_block(x, c, ada_w, ada_b, norm1_g, norm2_g, mlp_w1, mlp_w2,
              lru_w_in, lru_conv_w, lru_conv_b, lru_gate_a_w, lru_gate_a_b,
              lru_gate_x_w, lru_gate_x_b, lru_lambda, lru_w_out,
              kv_norm_g, kv_ada_w, kv_ada_b, kv_w, k_norm_g,
              attn_w_q, q_norm_g, rel_bias, attn_w_o):
    c_act = jax.nn.silu(c)
    h = x
    k_pad = None
    v_pad = None
    for layer in range(DEPTH):
        mod = c_act @ ada_w[layer] + ada_b[layer]
        sh1, sc1, g1, sh2, sc2, g2 = jnp.split(mod, 6, axis=-1)
        hn = modulate(rms_norm(h, norm1_g[layer]), sh1, sc1)
        if layer < N_A_LAYERS:
            y = recurrent_mixer(hn, lru_w_in[layer], lru_conv_w[layer], lru_conv_b[layer],
                                lru_gate_a_w[layer], lru_gate_a_b[layer],
                                lru_gate_x_w[layer], lru_gate_x_b[layer],
                                lru_lambda[layer], lru_w_out[layer])
        else:
            j = layer - N_A_LAYERS
            y = chunk_attention(hn, attn_w_q[j], q_norm_g[j], rel_bias[j], attn_w_o[j],
                                k_pad, v_pad)
        h = h + g1[:, None, :] * y
        hn = modulate(rms_norm(h, norm2_g[layer]), sh2, sc2)
        h = h + g2[:, None, :] * sqrelu_mlp(hn, mlp_w1[layer], mlp_w2[layer])
        if layer == N_A_LAYERS - 1:
            k_pad, v_pad = shared_kv(h, c_act, kv_norm_g, kv_ada_w, kv_ada_b, kv_w, k_norm_g)
    return h


PLE_DIM = 256
HEAD_DIM_2 = 64
DA_HEADS = 4
DA_V = 2 * HEAD_DIM_2
DA_QK = DA_HEADS * 2 * HEAD_DIM_2
DA_WIDTH = DA_HEADS * DA_V
MLA_HEADS = 8
MLA_NOPE = 64
MLA_ROPE = 32
MLA_V = 64
MLA_Q_RANK = 256
MLA_KV_RANK = 128
MLA_WIDTH = MLA_HEADS * MLA_V
SW_HEADS = 8
SW_KV_HEADS = 2
SW_GROUP = SW_HEADS // SW_KV_HEADS
SW_WINDOW = 128
SW_WIDTH = SW_HEADS * HEAD_DIM_2
N_BRANCHES = 3
REL_BUCKETS = 32
REL_MAX_DIST = 128
BIAS_HEADS = DA_HEADS + SW_HEADS
Q_BLOCK = 128
ROPE_THETA = 10000.0
NEG = -1e30

IN_SIZES = (DA_QK, DA_QK, DA_WIDTH, DA_WIDTH,
            MLA_Q_RANK, MLA_KV_RANK, MLA_ROPE, MLA_WIDTH,
            SW_HEADS * HEAD_DIM_2, SW_KV_HEADS * HEAD_DIM_2, SW_KV_HEADS * HEAD_DIM_2, SW_WIDTH,
            N_BRANCHES * D_MODEL)
IN_TOTAL = sum(IN_SIZES)


def rms_norm_2(x, w):
    xf = x.astype(jnp.float32)
    y = xf * lax.rsqrt(jnp.mean(xf * xf, axis=-1, keepdims=True) + EPS)
    return (y * w.astype(jnp.float32)).astype(x.dtype)

def rope(x, positions):
    half = x.shape[-1] // 2
    inv_freq = ROPE_THETA ** (-jnp.arange(half, dtype=jnp.float32) / half)
    ang = positions.astype(jnp.float32)[..., None] * inv_freq
    ang = ang.reshape(ang.shape[:2] + (1,) * (x.ndim - 3) + (half,))
    cos, sin = jnp.cos(ang), jnp.sin(ang)
    xf = x.astype(jnp.float32)
    x1, x2 = xf[..., :half], xf[..., half:]
    return jnp.concatenate([x1 * cos - x2 * sin, x2 * cos + x1 * sin], axis=-1).astype(x.dtype)

def t5_bucket(rel):
    n = jnp.maximum(rel, 0)
    max_exact = REL_BUCKETS // 2
    nf = jnp.maximum(n, 1).astype(jnp.float32)
    large = max_exact + (jnp.log(nf / max_exact) / math.log(REL_MAX_DIST / max_exact)
                         * (REL_BUCKETS - max_exact)).astype(jnp.int32)
    large = jnp.minimum(large, REL_BUCKETS - 1)
    return jnp.where(n < max_exact, n, large)

def sweep_query_blocks(block_fn, n_blocks):
    out = lax.map(block_fn, jnp.arange(n_blocks))
    out = jnp.moveaxis(out, 0, 1)
    return out.reshape((out.shape[0], n_blocks * Q_BLOCK) + out.shape[3:])

def diff_attention(q, k, v, lam, rel_table):
    S = q.shape[1]
    scale = HEAD_DIM_2 ** -0.5
    kf = k.astype(jnp.float32)
    table = rel_table.astype(jnp.float32)
    k_idx = jnp.arange(S)

    def block(i):
        q0 = i * Q_BLOCK
        qb = lax.dynamic_slice_in_dim(q, q0, Q_BLOCK, axis=1).astype(jnp.float32)
        s = jnp.einsum('bqhmd,bkhmd->bhmqk', qb, kf) * scale
        rel = (q0 + jnp.arange(Q_BLOCK))[:, None] - k_idx[None, :]
        bias = jnp.moveaxis(table[t5_bucket(rel)][..., :DA_HEADS], -1, 0)
        s = jnp.where(rel >= 0, s + bias[None, :, None], NEG)
        pm = jax.nn.softmax(s, axis=-1)
        w = pm[:, :, 0] - lam * pm[:, :, 1]
        return jnp.einsum('bhqk,bkhe->bqhe', w.astype(v.dtype), v)

    return sweep_query_blocks(block, S // Q_BLOCK)

def mla_attention(q_nope, q_rope, k_nope, k_rope, v):
    S = q_nope.shape[1]
    scale = (MLA_NOPE + MLA_ROPE) ** -0.5
    kn = k_nope.astype(jnp.float32)
    kr = k_rope.astype(jnp.float32)
    k_idx = jnp.arange(S)

    def block(i):
        q0 = i * Q_BLOCK
        qn = lax.dynamic_slice_in_dim(q_nope, q0, Q_BLOCK, axis=1).astype(jnp.float32)
        qr = lax.dynamic_slice_in_dim(q_rope, q0, Q_BLOCK, axis=1).astype(jnp.float32)
        s = (jnp.einsum('bqhd,bkhd->bhqk', qn, kn)
             + jnp.einsum('bqhr,bkr->bhqk', qr, kr)) * scale
        rel = (q0 + jnp.arange(Q_BLOCK))[:, None] - k_idx[None, :]
        s = jnp.where(rel >= 0, s, NEG)
        pm = jax.nn.softmax(s, axis=-1)
        return jnp.einsum('bhqk,bkhd->bqhd', pm.astype(v.dtype), v)

    return sweep_query_blocks(block, S // Q_BLOCK)

def sliding_window_attention(q, k, v, sinks, rel_table):
    B, S = q.shape[:2]
    nb = S // Q_BLOCK
    scale = HEAD_DIM_2 ** -0.5
    qb = q.reshape(B, nb, Q_BLOCK, SW_KV_HEADS, SW_GROUP, HEAD_DIM_2).astype(jnp.float32)

    def band(t):
        tp = jnp.pad(t, ((0, 0), (Q_BLOCK, 0), (0, 0), (0, 0)))
        tp = tp.reshape(B, nb + 1, Q_BLOCK, SW_KV_HEADS, HEAD_DIM_2)
        return jnp.concatenate([tp[:, :-1], tp[:, 1:]], axis=2)

    kb = band(k).astype(jnp.float32)
    vb = band(v)
    s = jnp.einsum('bnqhgd,bnkhd->bnhgqk', qb, kb) * scale
    qi = jnp.arange(Q_BLOCK)
    kj = jnp.arange(2 * Q_BLOCK)
    rel = Q_BLOCK + qi[:, None] - kj[None, :]
    bias = jnp.moveaxis(rel_table.astype(jnp.float32)[t5_bucket(rel)][..., DA_HEADS:], -1, 0)
    bias = bias.reshape(SW_KV_HEADS, SW_GROUP, Q_BLOCK, 2 * Q_BLOCK)
    in_window = (rel >= 0) & (rel < SW_WINDOW)
    key_valid = (jnp.arange(nb)[:, None] * Q_BLOCK + kj[None, :] - Q_BLOCK) >= 0
    mask = in_window[None] & key_valid[:, None, :]
    s = jnp.where(mask[None, :, None, None], s + bias, NEG)
    sink = jnp.broadcast_to(sinks.astype(jnp.float32).reshape(SW_KV_HEADS, SW_GROUP, 1, 1),
                            s.shape[:-1] + (1,))
    pm = jax.nn.softmax(jnp.concatenate([s, sink], axis=-1), axis=-1)[..., :-1]
    o = jnp.einsum('bnhgqk,bnkhd->bnqhgd', pm.astype(v.dtype), vb)
    return o.reshape(B, S, SW_WIDTH)

def second_inputs(seed: int = 0) -> dict:
    key = jax.random.key(seed)
    ks = jax.random.split(key, 24)
    f32 = jnp.float32

    def nrm(k, shape, scale):
        return jax.random.normal(k, shape, f32) * scale

    def gain(k, shape):
        return 1.0 + 0.05 * jax.random.normal(k, shape, f32)

    start = jax.random.randint(ks[2], (BATCH, 1), 0, 4096, dtype=jnp.int32)
    positions = start + jnp.arange(SEQ, dtype=jnp.int32)[None, :]
    return {
        "x": nrm(ks[0], (BATCH, SEQ, D_MODEL), 1.0),
        "p": nrm(ks[1], (DEPTH, BATCH, SEQ, PLE_DIM), 1.0),
        "positions": positions,
        "rel_bias": nrm(ks[3], (REL_BUCKETS, BIAS_HEADS), 0.3),
        "norm_pre": gain(ks[4], (DEPTH, D_MODEL)),
        "norm_post": gain(ks[5], (DEPTH, D_MODEL)),
        "w_in": nrm(ks[6], (DEPTH, D_MODEL, IN_TOTAL), D_MODEL ** -0.5),
        "da_lambda": nrm(ks[7], (DEPTH, 4, HEAD_DIM_2), 0.1),
        "da_subln": gain(ks[8], (DEPTH, DA_V)),
        "mla_q_norm": gain(ks[9], (DEPTH, MLA_Q_RANK)),
        "mla_w_qb": nrm(ks[10], (DEPTH, MLA_Q_RANK, MLA_HEADS * (MLA_NOPE + MLA_ROPE)), MLA_Q_RANK ** -0.5),
        "mla_kv_norm": gain(ks[11], (DEPTH, MLA_KV_RANK)),
        "mla_w_kvb": nrm(ks[12], (DEPTH, MLA_KV_RANK, MLA_HEADS * (MLA_NOPE + MLA_V)), MLA_KV_RANK ** -0.5),
        "sw_sinks": nrm(ks[13], (DEPTH, SW_HEADS), 0.5),
        "w_br_a": nrm(ks[14], (DEPTH, DA_WIDTH, D_MODEL), DA_WIDTH ** -0.5),
        "w_br_b": nrm(ks[15], (DEPTH, MLA_WIDTH, D_MODEL), MLA_WIDTH ** -0.5),
        "w_br_c": nrm(ks[16], (DEPTH, SW_WIDTH, D_MODEL), SW_WIDTH ** -0.5),
        "w_out": nrm(ks[17], (DEPTH, D_MODEL, D_MODEL), D_MODEL ** -0.5),
        "w_ple_gate": nrm(ks[18], (DEPTH, D_MODEL, D_MODEL), D_MODEL ** -0.5),
        "w_ple_proj": nrm(ks[19], (DEPTH, PLE_DIM, D_MODEL), PLE_DIM ** -0.5),
    }

def second_block(x, p, positions, rel_bias, norm_pre, norm_post, w_in, da_lambda, da_subln,
              mla_q_norm, mla_w_qb, mla_kv_norm, mla_w_kvb, sw_sinks,
              w_br_a, w_br_b, w_br_c, w_out, w_ple_gate, w_ple_proj):
    B, S, _ = x.shape
    split_points = tuple(int(c) for c in np.cumsum(IN_SIZES)[:-1])
    for l in range(DEPTH):
        h = rms_norm_2(x, norm_pre[l])
        u = h @ w_in[l]
        (a_q, a_k, a_v, a_z, b_q, b_kv, b_kr, b_z,
         c_q, c_k, c_v, c_z, g) = jnp.split(u, split_points, axis=-1)

        lam_init = 0.8 - 0.6 * math.exp(-0.3 * l)
        lf = da_lambda[l].astype(jnp.float32)
        lam = jnp.exp(jnp.sum(lf[0] * lf[1])) - jnp.exp(jnp.sum(lf[2] * lf[3])) + lam_init
        oa = diff_attention(a_q.reshape(B, S, DA_HEADS, 2, HEAD_DIM_2),
                            a_k.reshape(B, S, DA_HEADS, 2, HEAD_DIM_2),
                            a_v.reshape(B, S, DA_HEADS, DA_V), lam, rel_bias)
        oa = (rms_norm_2(oa, da_subln[l]) * (1.0 - lam_init)).reshape(B, S, DA_WIDTH)

        qm = (rms_norm_2(b_q, mla_q_norm[l]) @ mla_w_qb[l]).reshape(B, S, MLA_HEADS, MLA_NOPE + MLA_ROPE)
        q_nope, q_rope = qm[..., :MLA_NOPE], rope(qm[..., MLA_NOPE:], positions)
        kvm = (rms_norm_2(b_kv, mla_kv_norm[l]) @ mla_w_kvb[l]).reshape(B, S, MLA_HEADS, MLA_NOPE + MLA_V)
        k_nope, v_m = kvm[..., :MLA_NOPE], kvm[..., MLA_NOPE:]
        k_rope = rope(b_kr, positions)
        ob = mla_attention(q_nope, q_rope, k_nope, k_rope, v_m).reshape(B, S, MLA_WIDTH)

        oc = sliding_window_attention(c_q.reshape(B, S, SW_HEADS, HEAD_DIM_2),
                                      c_k.reshape(B, S, SW_KV_HEADS, HEAD_DIM_2),
                                      c_v.reshape(B, S, SW_KV_HEADS, HEAD_DIM_2),
                                      sw_sinks[l], rel_bias)

        gates = jax.nn.sigmoid(g).reshape(B, S, N_BRANCHES, D_MODEL)
        y = (gates[:, :, 0] * ((oa * jax.nn.silu(a_z)) @ w_br_a[l])
             + gates[:, :, 1] * ((ob * jax.nn.silu(b_z)) @ w_br_b[l])
             + gates[:, :, 2] * ((oc * jax.nn.silu(c_z)) @ w_br_c[l]))
        x = x + rms_norm_2(y @ w_out[l], norm_post[l])

        x = x + jax.nn.sigmoid(x @ w_ple_gate[l]) * (p[l] @ w_ple_proj[l])
    return x


def setup_inputs(seed=0):
    out = dict(first_inputs(seed))
    for name, value in second_inputs(seed + 1).items():
        if name != "x":
            out[name + "_2"] = value
    return out


def reference(
    x, c, ada_w, ada_b, norm1_g, norm2_g, mlp_w1, mlp_w2, lru_w_in, lru_conv_w, lru_conv_b,
    lru_gate_a_w, lru_gate_a_b, lru_gate_x_w, lru_gate_x_b, lru_lambda, lru_w_out, kv_norm_g,
    kv_ada_w, kv_ada_b, kv_w, k_norm_g, attn_w_q, q_norm_g, rel_bias, attn_w_o, p_2,
    positions_2, rel_bias_2, norm_pre_2, norm_post_2, w_in_2, da_lambda_2, da_subln_2,
    mla_q_norm_2, mla_w_qb_2, mla_kv_norm_2, mla_w_kvb_2, sw_sinks_2, w_br_a_2, w_br_b_2,
    w_br_c_2, w_out_2, w_ple_gate_2, w_ple_proj_2,
):
    x = first_block(
        x, c, ada_w, ada_b, norm1_g, norm2_g, mlp_w1, mlp_w2, lru_w_in, lru_conv_w, lru_conv_b,
        lru_gate_a_w, lru_gate_a_b, lru_gate_x_w, lru_gate_x_b, lru_lambda, lru_w_out,
        kv_norm_g, kv_ada_w, kv_ada_b, kv_w, k_norm_g, attn_w_q, q_norm_g, rel_bias, attn_w_o,
    )
    return second_block(
        x, p_2, positions_2, rel_bias_2, norm_pre_2, norm_post_2, w_in_2, da_lambda_2,
        da_subln_2, mla_q_norm_2, mla_w_qb_2, mla_kv_norm_2, mla_w_kvb_2, sw_sinks_2, w_br_a_2,
        w_br_b_2, w_br_c_2, w_out_2, w_ple_gate_2, w_ple_proj_2,
    )


_drawn_inputs = setup_inputs


def setup_inputs(seed=0):
    import zlib

    import numpy as np

    out = dict(_drawn_inputs(seed))
    spreads = {}
    factors = {'lru_gate_a_b': 8.0,
     'lru_gate_x_b': 8.0,
     'kv_norm_g': 5.972,
     'kv_ada_b': 7.373,
     'k_norm_g': 8.0,
     'q_norm_g': 8.0,
     'rel_bias': 3.472,
     'rel_bias_2': 2.78,
     'da_lambda_2': 4.979,
     'da_subln_2': 18.399,
     'mla_q_norm_2': 8.0,
     'mla_kv_norm_2': 3.44,
     'sw_sinks_2': 35.405,
     'norm_post_2': 3.658}
    for name, (base, spread) in spreads.items():
        noise = np.random.default_rng([zlib.crc32(name.encode()), seed]).standard_normal(out[name].shape)
        drawn = base * np.exp(spread * noise) if base else spread * noise
        out[name] = __import__('jax').numpy.asarray(drawn.astype(out[name].dtype))
    for name, factor in factors.items():
        out[name] = (out[name] * factor).astype(out[name].dtype)
    return out
```

```python
from contextlib import ExitStack, contextmanager
import math

import numpy as np

import concourse.bass as bass
from concourse import mybir

F32 = mybir.dt.float32
F32R = mybir.dt.float32r
I32 = mybir.dt.int32
ALU = mybir.AluOpType
ACT = mybir.ActivationFunctionType
AX = mybir.AxisListType.X

P = 128
T = 512
D = 1024
KD = D // P
NT = T // P
W = 1408
KW = W // P
LRU_BLK = 88
UB = 8
NEG = -1e30
EPS = 1e-6
LRU_C = 8.0
HD = 64
MLA_QK = 96
ROPE0 = 64
N_FF = 4
IN_OFF = dict(zip("aq ak av az bq bkv bkr bz cq ck cv cz g".split(),
                  np.cumsum([0, 512, 512, 512, 512, 256, 128, 32, 512, 512, 128, 128, 512]).tolist()))
TWO_PI = []
for _bits in (6, 15, 24):
    _part = round((2 * math.pi - sum(TWO_PI)) * 2 ** _bits) / 2 ** _bits
    TWO_PI.append(_part)
TWO_PI.append(2 * math.pi - sum(TWO_PI))
PI_IN = float(np.nextafter(np.float32(math.pi), np.float32(0)))
N_ADA = 56
ADA_FIRST = 8

VEC = {}
_at = 0
for _name, _n in [("c", 8), ("ada_b", 112), ("norm1_g", 16), ("norm2_g", 16), ("kv_norm_g", 8),
                  ("conv_w", 44), ("conv_b", 11), ("ga_b", 11), ("gx_b", 11), ("lam", 11),
                  ("k_g", 1), ("q_g", 1), ("pre_g", 16), ("post_g", 16), ("mq_g", 4), ("mkv_g", 2),
                  ("subln", 2), ("sinks", 16), ("da_l", 512), ("inv_freq", 1), ("eps", 1)]:
    VEC[_name] = _at
    _at += _n
NVEC = _at


def lru_tiles(j):
    first, last = P * j // LRU_BLK, (P * (j + 1) - 1) // LRU_BLK
    return list(range(LRU_BLK * first // P, (LRU_BLK * (last + 1) - 1) // P + 1))


class Lane:

    def __init__(self, name, eng, sem, plan):
        self.name, self.e, self.sem, self.plan = name, eng, sem, plan
        self.total, self.local, self.in_loop, self.i = 0, 0, None, None

    @contextmanager
    def loop(self, n):
        self.in_loop, self.local = f"{self.name}{self.total}_{self.plan['n']}", 0
        self.plan["n"] += 1
        with self.e.Fori(0, n) as i:
            self.i = i
            yield i
        self.plan["per_iteration"][self.in_loop] = self.local
        self.total += n * self.local
        self.in_loop, self.i, self.local = None, None, 0

    def done(self, ins, ev):
        ins.then_inc(self.sem, 1)
        if self.in_loop is None:
            self.total += 1
        else:
            self.local += 1
        self.plan["events"][ev] = (self.name, self.total + self.local, self.in_loop)


def build(nc, io, plan, counted):
    ctx = ExitStack()
    with ctx:
        def sb(name, shape, dt=F32):
            return ctx.enter_context(nc.sbuf_tensor(name, shape, dt))

        def sem(name):
            return ctx.enter_context(nc.semaphore(name))

        h = sb("h", [P, KD, T])
        xh, xl = sb("xh", [P, KD, T], F32R), sb("xl", [P, KD, T], F32R)
        bh, bl = sb("bh", [P, KW, T], F32R), sb("bl", [P, KW, T], F32R)
        bC, bD, bT = sb("bC", [P, KW, T]), sb("bD", [P, KW, T]), sb("bT", [P, KW, T])
        bS = sb("bS", [P, 4, T])
        raw = [sb(f"raw{p}", [P, UB, P]) for p in range(2)]
        wh = [sb(f"wh{p}", [P, UB, P], F32R) for p in range(2)]
        wl = [sb(f"wl{p}", [P, UB, P], F32R) for p in range(2)]
        bA = sb("bA", [P, 4, T])
        acc = sb("acc", [P, 256])
        vec = sb("vec", [P, NVEC])
        cst = sb("cst", [P, 4, P])
        mod = sb("mod", [P, 112])
        gs = sb("gs", [P, 5, KD])
        sm = sb("sm", [P, 64])
        ps = [ctx.enter_context(nc.psum_tensor(f"ps{b}", [P, T], F32)) for b in range(8)]
        ident, ones, ones64, swap = (cst[:, k, :] for k in range(4))
        SC, SLAM, SBA, SBX, SNM, SRS, SES, SRI, SLN, SSQ = 0, 8, 19, 30, 41, 45, 49, 53, 57, 60

        s_raw = [sem(f"s_raw{p}") for p in range(2)]
        s_hi, s_lo = sem("s_hi"), sem("s_lo")
        s_unit = sem("s_unit")
        s_bank = [sem(f"s_bank{b}") for b in range(4)]
        s_par = sem("s_par")
        s_a0 = [sem(f"s_a0{k}") for k in range(ADA_FIRST)]
        s_ada = sem("s_ada")
        s_aux = sem("s_aux")
        s_bias = sem("s_bias")
        s_out = sem("s_out")
        s_apart = sem("s_apart")
        s_score = sem("s_score")
        s_sread = sem("s_sread")
        s_nm = sem("s_nm")
        s_exp = sem("s_exp")
        s_w = sem("s_w")
        s_t = sem("s_t")
        s_pt = sem("s_pt")
        s_pv = sem("s_pv")
        s_o = sem("s_o")
        sems = {n: sem(f"lane_{n}") for n in ("pe", "act", "dve", "pool", "sp")}
        block = ctx.enter_context(nc.Block())

        def v(name, k=0, n=1):
            return vec[:, VEC[name] + k:VEC[name] + k + n]

        def vdyn(name, k, n=1):
            return vec[:, bass.ds(VEC[name] + k, n)]

        def program(L):
            pe, act, dve, pool, sp = (L.name == n for n in ("pe", "act", "dve", "pool", "sp"))
            e = L.e
            done = L.done
            U = [0]
            BK = [0, 0, 0, 0]
            NX, NS, NB, NW, AT = [0], [0], [0], [0], [0]
            NA = [0]

            def need(ev, it=None):
                who, value, in_loop = counted["events"].get(ev, ("dve", 1, None))
                if in_loop is not None:
                    value = value + (L.i if it is None else it) * counted["per_iteration"][in_loop]
                e.wait_ge(sems[who], value)

            def loop(n, *lanes):
                return L.loop(n) if L.name in lanes else _skip()

            def place(u0, it, q):
                return (u0 + q) % 2, (u0 + q) // 2 + it

            def split(u0, it, q):
                p, k = place(u0, it, q)
                if act:
                    e.wait_ge(s_raw[p], 16 * (k + 1))
                    e.wait_ge(s_unit, 2 * k + p - 1)
                    e.activation(wh[p][:], raw[p][:], ACT.Copy).then_inc(s_hi, 1)
                if dve:
                    e.wait_ge(s_hi, 2 * k + p + 1)
                    e.tensor_tensor(wl[p][:], raw[p][:], wh[p][:].bitcast(F32), ALU.subtract)\
                     .then_inc(s_lo, 1)

            def mm3(out, p, blk, xhi, xlo, start, stop, M=P):
                e.matmul(out, wl[p][:, blk, 0:M], xhi, start=start, stop=False)
                e.matmul(out, wh[p][:, blk, 0:M], xlo, start=False, stop=False)
                return e.matmul(out, wh[p][:, blk, 0:M], xhi, start=False, stop=stop)

            def unit_pe(u0, it, q, parts, before=None):
                if not pe:
                    return
                p, k = place(u0, it, q)
                e.wait_ge(s_lo, 2 * k + p + 1)
                for bank, used, blks, tiles, (hi, lo) in parts:
                    e.wait_ge(s_bank[bank], used + 1)
                    for n, (blk, kt) in enumerate(zip(blks, tiles)):
                        if before is not None:
                            before(kt)
                        mm = mm3(ps[bank][:], p, blk, hi[:, kt, :], lo[:, kt, :], n == 0, n == len(blks) - 1)
                mm.then_inc(s_unit, 1)

            def unit_read(u0, it, q):
                e.wait_ge(s_unit, u0 + 2 * it + q + 1)

            FULL = (range(UB), range(KD))

            def apart():
                e.sem_inc(s_apart, 1)

            def ada_sum(src, ev):
                done(e.tensor_scalar(acc[:], src[:, 0, :], sm[:, SC:SC + 1], None, ALU.mult), ev + "0")
                for k in range(1, KD):
                    need(f"{ev}{k - 1}")
                    done(e.scalar_tensor_tensor(acc[:], src[:, k, :], sm[:, SC + k:SC + k + 1], acc[:],
                                                ALU.mult, ALU.add), f"{ev}{k}")

            panel = bA[:].rearrange("p a b -> p (a b)").rearrange("p (k n) -> p k n", k=KD)

            def ada_load(a):
                e.dma_start(panel, io["ada"][a]).then_inc(s_ada, 16)

            def ada_begin(s, a):
                if dve:
                    e.wait_ge(s_ada, 16 * (a - (ADA_FIRST - 1)))
                    ada_sum(panel, s + "acc")

            def ada_pe(s):
                if pe:
                    need(f"{s}acc{KD - 1}")
                    for c in range(2):
                        mm = e.matmul(ps[6][:, c:c + 1], acc[:, P * c:P * c + P], ones[:, 0:1],
                                      start=True, stop=True)
                    done(mm, s + "adamm")

            def ada_end(s, a):
                if dve:
                    need(s + "adamm")
                    done(e.tensor_tensor(mod[:, bass.ds(2 * a, 2)] if not isinstance(a, int) else mod[:, 2 * a:2 * a + 2],
                                         ps[6][:, 0:2],
                                         vdyn("ada_b", 2 * a, 2) if not isinstance(a, int) else v("ada_b", 2 * a, 2),
                                         ALU.add), s + "mod")
                if act:
                    need(f"{s}acc{KD - 1}")
                    ada_load(a + 1)

            def stats(s, src, n, width, sq, out, free):
                if act:
                    for ev in free:
                        need(*ev)
                    for k in range(n):
                        done(e.activation(sq(k), src(k), ACT.Square), f"{s}sq{k}")
                if pe:
                    for k in range(n):
                        need(f"{s}sq{k}")
                        mm = e.matmul(ps[7][:], ones, sq(k), start=(k == 0), stop=(k == n - 1))
                    done(mm, s + "sum")
                if act:
                    need(s + "sum")
                    done(e.activation(out, ps[7][:], ACT.Sqrt, scale=1.0 / width, bias=v("eps")), s + "root")
                if dve:
                    need(s + "root")
                    done(e.reciprocal(out, out), s + "rstd")

            def put(s, k, src, hi, lo, scale=1.0):
                if act:
                    need(f"{s}y{k}")
                    if L.in_loop:
                        apart()
                    done(e.activation(hi, src, ACT.Copy), f"{s}hi{k}")
                if pool:
                    need(f"{s}hi{k}")
                    done(e.tensor_tensor(lo, src, hi.bitcast(F32), ALU.subtract), f"{s}lo{k}")

            def norm(s, src, n, width, gain, shift, hi, lo, free, tmp, rstd, fresh=True):
                if fresh:
                    stats(s, src, n, width, tmp, rstd, free)
                for k in range(n):
                    if dve:
                        if k == 0 and fresh:
                            need(s + "rstd")
                        if k == 0:
                            for ev in free:
                                need(*ev)
                        done(e.tensor_tensor(tmp(k), src(k), rstd, ALU.mult), f"{s}t{k}")
                        need(f"{s}t{k}")
                        done(e.tensor_scalar(tmp(k), tmp(k), gain(k), shift(k) if shift else None,
                                             ALU.mult, ALU.add if shift else ALU.bypass), f"{s}y{k}")
                    if act and k == 0:
                        e.wait_ge(s_unit, U[0])
                    put(s, k, tmp(k), hi[:, k, :], lo[:, k, :])

            def hk(k):
                return h[:, k, :]

            def last(s, k=None):
                if pe:
                    need(f"{s}lo{k}")

            def mod_gain(s, n, col, g):
                if dve:
                    done(e.scalar_tensor_tensor(gs[:, n, :], mod[:, col:col + KD], 1.0, g, ALU.add, ALU.mult), s + "gs")
                    need(s + "gs")

            flat = lambda ap: ap.rearrange("p a b -> p (a b)")
            first = [flat(bA[:])] + [flat(b[:, 4 * q:4 * q + 4, :]) for b in (bC, bD, bT) for q in range(2)] \
                + [flat(h[:, 0:4, :])]
            if sp:
                e.dma_start(vec[:], io["vec"]).then_inc(s_par, 16)
                e.dma_start(cst[:], io["cst"]).then_inc(s_par, 16)
                for a in range(ADA_FIRST):
                    e.dma_start(first[a], io["ada"][a].rearrange("p a b -> p (a b)")).then_inc(s_a0[a], 16)
                for k in range(2):
                    e.dma_start(raw[k][:], io["w"][k]).then_inc(s_raw[k], 16)
                need(f"i7acc{KD - 1}")
                e.dma_start(h[:], io["x"]).then_inc(s_par, 16)
            if pe:
                for s_ in (*s_bank, s_score):
                    e.sem_inc(s_, 1)
                for s_ in (s_sread, s_exp, s_t, s_pt, s_pv, s_o):
                    e.sem_inc(s_, 2)
            if act:
                e.wait_ge(s_par, 32)
                done(e.activation(sm[:, SC:SC + 8], v("c", 0, 8), ACT.Tanh, scale=0.5), "i_th")
                done(e.activation(sm[:, SLAM:SLAM + KW], v("lam", 0, KW), ACT.Exp, scale=-1.0), "i_el")
                need("i_el")
                done(e.activation(sm[:, SLAM:SLAM + KW], sm[:, SLAM:SLAM + KW], ACT.Ln, bias=ones[:, 0:1]), "i_sp")
            if dve:
                e.wait_ge(s_par, 32)
                need("i_th")
                done(e.scalar_tensor_tensor(sm[:, SC:SC + 8], sm[:, SC:SC + 8], 1.0, v("c", 0, 8), ALU.add, ALU.mult), "i_c1")
                need("i_c1")
                done(e.tensor_scalar(sm[:, SC:SC + 8], sm[:, SC:SC + 8], 0.5, None, ALU.mult), "i_c")
                need("i_sp")
                done(e.tensor_scalar(sm[:, SLAM:SLAM + KW], sm[:, SLAM:SLAM + KW], -LRU_C / 2, None, ALU.mult), "i_nsp")
                done(e.tensor_scalar(sm[:, SBA:SBA + KW], v("ga_b", 0, KW), 0.5, None, ALU.mult), "i_ba")
                done(e.tensor_scalar(sm[:, SBX:SBX + KW], v("gx_b", 0, KW), 0.5, None, ALU.mult), "i_bx")
                need("i_bx")
            if pe:
                e.wait_ge(s_par, 32)
            for a in range(ADA_FIRST):
                if dve:
                    e.wait_ge(s_a0[a], 16)
                    if a:
                        need(f"i{a - 1}mod")
                    ada_sum(first[a].rearrange("p (k n) -> p k n", k=KD), f"i{a}acc")
                ada_pe(f"i{a}")
                if dve:
                    need(f"i{a}adamm")
                    done(e.tensor_tensor(mod[:, 2 * a:2 * a + 2], ps[6][:, 0:2], v("ada_b", 2 * a, 2), ALU.add), f"i{a}mod")
                if act and a == 0:
                    need(f"i0acc{KD - 1}")
                    ada_load(ADA_FIRST)
            if dve:
                need(f"i{ADA_FIRST - 1}mod")
            mod_gain("n0", 0, 8, v("norm1_g", 0, 8))
            for q in range(2):
                if act:
                    e.wait_ge(s_raw[q], 16)
                    e.activation(wh[q][:], raw[q][:], ACT.Copy).then_inc(s_hi, 1)
                if dve:
                    e.wait_ge(s_hi, q + 1)
                    e.tensor_tensor(wl[q][:], raw[q][:], wh[q][:].bitcast(F32), ALU.subtract).then_inc(s_lo, 1)
            if act or dve:
                e.wait_ge(s_par, 48)
            bTk = lambda k: bT[:, k, :]
            norm("n0", hk, KD, D, lambda k: gs[:, 0, k:k + 1], lambda k: mod[:, k:k + 1], xh, xl,
                 [(f"i7acc{KD - 1}",), ("n0gs",)], bTk, bT[:, 9, :])

            if sp:
                with L.loop(io["units"] // 2 - 1) as i:
                    for p in range(2):
                        e.wait_ge(s_lo, 2 * i + p + 1)
                        e.dma_start(raw[p][:], io["w"][2 * i + (2 + p)]).then_inc(s_raw[p], 16)

            u0, b0, b1 = U[0], BK[0], BK[1]
            last("n0", KD - 1)
            with loop(KW, "pe", "act", "dve", "pool") as it:
                if dve:
                    ada_begin("A", ADA_FIRST + it)
                unit_pe(u0, it, 0, [(0, b0 + it if pe else 0, *FULL, (xh, xl))])
                unit_pe(u0, it, 1, [(1, b1 + it if pe else 0, *FULL, (xh, xl))])
                ada_pe("A")
                if act:
                    unit_read(u0, it, 0)
                if act or dve:
                    split(u0 + 2, it, 0)
                if act:
                    need("Aconv0", it - 1)
                    e.activation(bS[:, 0, :], ps[0][:], ACT.Copy).then_inc(s_bank[0], 1)
                if dve:
                    e.wait_ge(s_bank[0], b0 + it + 2)
                    done(e.tensor_scalar(bD[:, it, :], bS[:, 0, :], vdyn("conv_w", it + 3 * KW), vdyn("conv_b", it + 0),
                                         ALU.mult, ALU.add), "Aconv3")
                    for j in (2, 1, 0):
                        need(f"Aconv{j + 1}")
                        done(e.scalar_tensor_tensor(bD[:, it, 3 - j:T], bS[:, 0, 0:T - 3 + j], vdyn("conv_w", it + j * KW),
                                                    bD[:, it, 3 - j:T], ALU.mult, ALU.add), f"Aconv{j}")
                if act:
                    unit_read(u0, it, 1)
                if act or dve:
                    split(u0 + 2, it, 1)
                if act:
                    need("Agelu", it - 1)
                    e.activation(bS[:, 1, :], ps[1][:], ACT.Copy).then_inc(s_bank[1], 1)
                    e.wait_ge(s_bank[1], b1 + it + 2)
                    done(e.activation(bS[:, 2, :], bS[:, 1, :], ACT.Square), "Ax2")
                    need("Aconv0")
                    apart()
                    done(e.activation(bh[:, it, :], bD[:, it, :], ACT.Copy), "Ahi")
                if pool:
                    need("Ahi")
                    done(e.tensor_tensor(bl[:, it, :], bD[:, it, :], bh[:, it, :].bitcast(F32), ALU.subtract), "Alo")
                if dve:
                    need("Ax2")
                    done(e.tensor_scalar(bS[:, 2, :], bS[:, 2, :], 0.044715, 1.0, ALU.mult, ALU.add), "Ai1")
                    need("Ai1")
                    done(e.scalar_tensor_tensor(bS[:, 2, :], bS[:, 2, :], math.sqrt(2 / math.pi), bS[:, 1, :],
                                                ALU.mult, ALU.mult), "Ai2")
                if act:
                    need("Ai2")
                    done(e.activation(bS[:, 3, :], bS[:, 2, :], ACT.Tanh), "Ath")
                if dve:
                    need("Ath")
                    done(e.scalar_tensor_tensor(bC[:, it, :], bS[:, 3, :], 1.0, bS[:, 1, :], ALU.add, ALU.mult), "Agelu")
                if dve or act:
                    ada_end("A", ADA_FIRST + it)
            U[0] += 2 * KW
            BK[0] += KW
            BK[1] += KW

            if dve:
                e.wait_ge(s_ada, 16 * (KW + 1))
                ada_sum(panel, "Bacc")
            ada_pe("B")
            if dve:
                a = ADA_FIRST + KW
                need("Badamm")
                done(e.tensor_tensor(mod[:, 2 * a:2 * a + 2], ps[6][:, 0:2], v("ada_b", 2 * a, 2), ALU.add), "Bmod")
            u0 = U[0]
            groups = [list(range(g, min(g + 4, KW))) for g in range(0, KW, 4)]
            if act or pe:
                need("Alo", KW - 1)
                need("Agelu", KW - 1)
            for j in range(KW):
                ks = lru_tiles(j)
                ba, bx = j % 2, 2 + j % 2
                unit_pe(u0, 0, j, [(bk, BK[bk], [3 * g + k - j + 1 for k in ks], ks, (bh, bl))
                                   for g, bk in enumerate((ba, bx))])
                if act:
                    unit_read(u0, 0, j)
                split(u0 + 2, 0, j)
                t1, t2, sq = bS[:, j % 2, :], bS[:, 2 + j % 2, :], bA[:, j % 4, :]
                a, x = bT[:, j, :], bD[:, j, :]
                nsp = sm[:, SLAM + j:SLAM + j + 1]
                if act:
                    if j >= 2:
                        need(f"G{j - 2}v")
                    e.activation(t1, ps[ba][:], ACT.Tanh, scale=0.5, bias=sm[:, SBA + j:SBA + j + 1]).then_inc(s_bank[ba], 1)
                    e.activation(t2, ps[bx][:], ACT.Tanh, scale=0.5, bias=sm[:, SBX + j:SBX + j + 1]).then_inc(s_bank[bx], 1)
                    e.wait_ge(s_bank[ba], BK[ba] + 2)
                    done(e.activation(a, t1, ACT.Exp, scale=nsp, bias=nsp), f"G{j}a")
                    need(f"G{j}a")
                    done(e.activation(t1, t1, ACT.Tanh, scale=nsp, bias=nsp), f"G{j}th")
                if dve:
                    need(f"G{j}th")
                    e.wait_ge(s_bank[bx], BK[bx] + 2)
                    if j >= 4:
                        need(f"G{j - 4}u")
                    done(e.tensor_tensor(sq, a, a, ALU.mult), f"G{j}aa")
                    need(f"G{j}aa")
                    done(e.scalar_tensor_tensor(sq, sq, 1.0, t1, ALU.add, ALU.mult), f"G{j}q")
                    done(e.scalar_tensor_tensor(x, t2, 1.0, x, ALU.add, ALU.mult), f"G{j}v")
                BK[ba] += 1
                BK[bx] += 1
                for g in groups:
                    if g[-1] != j:
                        continue
                    if act:
                        for m in g:
                            need(f"G{m}q")
                            done(e.activation(bA[:, m % 4, :], bA[:, m % 4, :], ACT.Sqrt, scale=-0.25), f"G{m}s")
                    if dve:
                        for m in g:
                            need(f"G{m}s")
                            done(e.tensor_tensor(bD[:, m, :], bD[:, m, :], bA[:, m % 4, :], ALU.mult), f"G{m}u")
                            need(f"G{m}u")
                            done(e.tensor_tensor_scan(bT[:, m, :], bT[:, m, :], bD[:, m, :], 0.0, ALU.mult, ALU.add), f"G{m}r")
                            need(f"G{m}r")
                            done(e.scalar_tensor_tensor(bC[:, m, :], bC[:, m, :], 0.5, bT[:, m, :], ALU.mult, ALU.mult), f"Yy{m}")
            U[0] += KW
            if act:
                need(f"G{KW - 1}u")
                ada_load(ADA_FIRST + KW + 1)
                e.wait_ge(s_unit, U[0])
            for j in range(KW):
                put("Y", j, bC[:, j, :], bh[:, j, :], bl[:, j, :])

            u0 = U[0]
            used = [BK[0], BK[1]]
            for j in range(KW):
                if pe:
                    p, k = place(u0, 0, j)
                    if j == 0:
                        need(f"Ylo{KW - 1}")
                    e.wait_ge(s_lo, 2 * k + p + 1)
                    for blk in range(UB):
                        m, kt = divmod(UB * j + blk, KW)
                        bk = m % 2
                        if kt == 0:
                            e.wait_ge(s_bank[bk], used[bk] + m // 2 + 1)
                        mm = mm3(ps[bk][:], p, blk, bh[:, kt, :], bl[:, kt, :], kt == 0, kt == KW - 1)
                        if kt == KW - 1 and blk < UB - 1:
                            done(mm, f"Op{m}")
                    mm.then_inc(s_unit, 1)
                split(u0 + 2, 0, j)
                for blk in range(UB):
                    m, kt = divmod(UB * j + blk, KW)
                    if kt == KW - 1 and dve:
                        if blk < UB - 1:
                            need(f"Op{m}")
                        else:
                            unit_read(u0, 0, j)
                        e.scalar_tensor_tensor(h[:, m, :], ps[m % 2][:], mod[:, 16 + m:17 + m], h[:, m, :],
                                               ALU.mult, ALU.add).then_inc(s_bank[m % 2], 1)
                if j < 4:
                    a = ADA_FIRST + KW + 1 + j
                    if dve:
                        e.wait_ge(s_ada, 16 * (KW + 2 + j))
                        ada_sum(panel, f"O{j}acc")
                    ada_pe(f"O{j}")
                    ada_end(f"O{j}", a)
            U[0] += KW
            BK[0] += KD // 2
            BK[1] += KD // 2

            def h_ready():
                if act or dve:
                    e.wait_ge(s_bank[0], BK[0] + 1)
                    e.wait_ge(s_bank[1], BK[1] + 1)

            def mlp(s, g2, ada0):
                u0, b = U[0], list(BK)
                last(s + "n", KD - 1)
                with loop(N_FF, "pe", "act", "dve", "pool") as c:
                    it0 = UB * c if L.name in ("pe", "act", "dve") else 0
                    for n in range(2 * KD):
                        up, it, q = n < KD, (it0 + n // 2), n % 2
                        if ada0 is not None and q == 0 and dve:
                            ada_begin(f"{s}{n}", ada0 + it)
                        if up:
                            unit_pe(u0, it, q, [(q, b[q] + it if pe else 0, *FULL, (xh, xl))])
                        else:
                            unit_pe(u0, it, q, [(q, b[q] + it if pe else 0, *FULL, (bh, bl))],
                                    before=(lambda kt: need(f"{s}lo{kt}")) if n == KD else None)
                        if act or (dve and not up):
                            unit_read(u0, it, q)
                        if act or dve:
                            split(u0 + 2, it, q)
                        if up:
                            if act:
                                need(f"{s}y{(n - 2) % KD}", c - (n < 2))
                                e.activation(bS[:, q, :], ps[q][:], ACT.Relu).then_inc(s_bank[q], 1)
                            if dve:
                                e.wait_ge(s_bank[q], b[q] + it + 2)
                                need(f"{s}lo{(n - 2) % KD}", c - (n < 2))
                                done(e.tensor_tensor(bS[:, 2 + q, :], bS[:, q, :], bS[:, q, :], ALU.mult), f"{s}y{n}")
                            put(s, n, bS[:, 2 + q, :], bh[:, n, :], bl[:, n, :])
                        elif dve:
                            m = n - KD
                            e.scalar_tensor_tensor(h[:, m, :], ps[q][:], mod[:, g2 + m:g2 + m + 1], h[:, m, :],
                                                   ALU.mult, ALU.add).then_inc(s_bank[q], 1)
                        if ada0 is not None and q == 1:
                            t = f"{s}{n - 1}"
                            ada_pe(t)
                            if dve or act:
                                ada_end(t, ada0 + it)
                U[0] += 2 * KD * N_FF
                for q in range(2):
                    BK[q] += KD * N_FF

            def norm_mod(s, n, src_cols, gain, extra=(), region=bTk, rstd=bT[:, 9, :], fresh=True):
                sh, sc = src_cols
                h_ready()
                mod_gain(s, n, sc, gain)
                norm(s, hk, KD, D, lambda k: gs[:, n, k:k + 1], lambda k: mod[:, sh + k:sh + k + 1], xh, xl,
                     list(extra), region, rstd, fresh)

            norm_mod("M0n", 1, (24, 32), v("norm2_g", 0, 8), [("O3mod",), (f"Yy{KW - 1}",)])
            mlp("M0", 40, ADA_FIRST + KW + 5)
            o_tok = bD[:, 8, :].rearrange("p (i f) -> p i f", i=NT)
            o_feat, scratch = bD[:, 9, :], bD[:, 10, :]

            def attend(steps, it, before=0, parts=1):
                AT[0] += 1
                at = f"at{AT[0]}"
                nx, ns = sum(len(st["q"]) for st in steps), len(steps)
                x0 = NX[0] + nx * before + nx * parts * it
                s0 = NS[0] + ns * before + ns * parts * it
                w0 = NW[0] + ns * before + ns * parts * it
                xs = [i * (nx // ns) for i in range(ns)]

                def scores(n):
                    st = steps[n]
                    for m in range(len(st["q"])):
                        x = xs[n] + m
                        e.wait_ge(s_sread, x0 + (x + 1))
                        e.matmul(ps[2 + x % 2][:, 0:st["nk"]], st["q"][m], st["k"][m], start=True, stop=True)\
                         .then_inc(s_score, 1)

                def maximum(n):
                    st = steps[n]
                    for m in range(len(st["q"])):
                        x = xs[n] + m
                        sc, nm = bD[:, x % 2, 0:st["nk"]], sm[:, SNM + x % 4:SNM + x % 4 + 1]
                        e.wait_ge(s_score, x0 + (x + 2))
                        e.wait_ge(s_exp, x0 + (x + 1))
                        e.scalar_tensor_tensor(sc, ps[2 + x % 2][:, 0:st["nk"]], st["scale"], st["bias"],
                                               ALU.mult, ALU.add).then_inc(s_sread, 1)
                        e.wait_ge(s_sread, x0 + (x + 3))
                        done(e.tensor_reduce(nm, sc, AX, ALU.max), f"{at}_{n}{m}mx")
                        need(f"{at}_{n}{m}mx")
                        if st.get("sink") is not None:
                            i = e.tensor_scalar(nm, nm, st["sink"], -1.0, ALU.max, ALU.mult)
                        else:
                            i = e.tensor_scalar(nm, nm, -1.0, None, ALU.mult)
                        i.then_inc(s_nm, 1)

                def exponentials(n):
                    st = steps[n]
                    e.wait_ge(s_t, s0 + (n + 1))
                    for m in range(len(st["q"])):
                        x = xs[n] + m
                        c = x % 4
                        e.wait_ge(s_nm, x0 + (x + 1))
                        nm = sm[:, SNM + c:SNM + c + 1]
                        if st.get("sink") is not None:
                            apart()
                            done(e.activation(sm[:, SES + c:SES + c + 1], st["sink"], ACT.Exp, bias=nm), f"{at}_{n}es")
                        e.activation(bD[:, 2 + c, 0:st["nk"]], bD[:, x % 2, 0:st["nk"]], ACT.Exp, bias=nm,
                                     accum_out=sm[:, SRS + c:SRS + c + 1]).then_inc(s_exp, 1)

                def combine(n):
                    st = steps[n]
                    x = xs[n]
                    c = x % 4
                    e.wait_ge(s_exp, x0 + (x + 4))
                    ri = sm[:, SRI + c:SRI + c + 2]
                    done(e.reciprocal(ri, sm[:, SRS + c:SRS + c + 2]), f"{at}_{n}ri")
                    need(f"{at}_{n}ri")
                    p0, p1 = bD[:, 2 + c, 0:st["nk"]], bD[:, 3 + c, 0:st["nk"]]
                    done(e.tensor_scalar(p0, p0, ri[:, 0:1], None, ALU.mult), f"{at}_{n}p0")
                    done(e.tensor_scalar(ri[:, 1:2], ri[:, 1:2], st["lam"], None, ALU.mult), f"{at}_{n}lm")
                    need(f"{at}_{n}lm")
                    e.scalar_tensor_tensor(p0, p1, ri[:, 1:2], p0, ALU.mult, ALU.add).then_inc(s_w, 1)

                def turn(n):
                    st = steps[n]
                    x = xs[n]
                    if st.get("lam") is not None:
                        e.wait_ge(s_w, w0 + (n + 1))
                    else:
                        e.wait_ge(s_exp, x0 + (x + 3))
                    e.wait_ge(s_pt, s0 + (n + 1))
                    for b in range(st["nk"] // P):
                        mm = e.transpose(ps[4 + n % 2][:, P * b:P * b + P],
                                         bD[:, 2 + x % 4, P * b:P * b + P], ident)
                    mm.then_inc(s_t, 1)

                def turned(n):
                    st = steps[n]
                    e.wait_ge(s_t, s0 + (n + 3))
                    e.wait_ge(s_pv, s0 + (n + 1))
                    e.activation(bD[:, 6 + n % 2, 0:st["nk"]], ps[4 + n % 2][:, 0:st["nk"]], ACT.Copy)\
                     .then_inc(s_pt, 1)

                def values(n):
                    st = steps[n]
                    e.wait_ge(s_pt, s0 + (n + 3))
                    e.wait_ge(s_o, s0 + (n + 1))
                    nb = st["nk"] // P
                    for b in range(nb):
                        mm = e.matmul(ps[6 + n % 2][:, 0:st["dv"]], bD[:, 6 + n % 2, P * b:P * b + P], st["v"][b],
                                      start=(b == 0), stop=(b == nb - 1))
                    mm.then_inc(s_pv, 1)

                def results(n):
                    st = steps[n]
                    x = xs[n]
                    c = x % 4
                    src = ps[6 + n % 2][:, 0:st["dv"]]
                    if st.get("lam") is not None:
                        e.wait_ge(s_pv, s0 + (n + 3))
                        e.tensor_copy(st["o"], src).then_inc(s_o, 1)
                        return
                    rs, ri = sm[:, SRS + c:SRS + c + 1], sm[:, SRI + c:SRI + c + 1]
                    e.wait_ge(s_exp, x0 + (x + 3))
                    if st.get("sink") is not None:
                        done(e.tensor_tensor(rs, rs, sm[:, SES + c:SES + c + 1], ALU.add), f"{at}_{n}sk")
                        need(f"{at}_{n}sk")
                    done(e.reciprocal(ri, rs), f"{at}_{n}ri")
                    need(f"{at}_{n}ri")
                    e.wait_ge(s_pv, s0 + (n + 3))
                    e.tensor_scalar(st["o"], src, ri, None, ALU.mult).then_inc(s_o, 1)

                if pe:
                    scores(0)
                if dve:
                    maximum(0)
                for n in range(ns):
                    if pe:
                        if n + 1 < ns:
                            scores(n + 1)
                        turn(n)
                        if n:
                            values(n - 1)
                    if act:
                        exponentials(n)
                        if n:
                            turned(n - 1)
                    if dve:
                        if n + 1 < ns:
                            maximum(n + 1)
                        if steps[n].get("lam") is not None:
                            combine(n)
                        if n:
                            results(n - 1)
                if pe:
                    values(ns - 1)
                if act:
                    turned(ns - 1)
                if dve:
                    results(ns - 1)

            def attended(steps, times):
                NX[0] += sum(len(st["q"]) for st in steps) * times
                NS[0] += len(steps) * times
                if steps[0].get("lam") is not None:
                    NW[0] += len(steps) * times

            def copy_out(bank, used, dst):
                if act:
                    e.activation(dst, ps[bank][:], ACT.Copy).then_inc(s_bank[bank], 1)

            def copied(bank, used):
                e.wait_ge(s_bank[bank], used + 2)

            def head_norm(s, bank, used, x, tmp, gain, out):
                if act:
                    copied(bank, used)
                    apart()
                    done(e.activation(tmp, x, ACT.Square), s + "hsq")
                if pe:
                    need(s + "hsq")
                    done(e.matmul(ps[bank][:], ones64, tmp, start=True, stop=True), s + "hsum")
                if act:
                    need(s + "hsum")
                    e.activation(tmp, ps[bank][:], ACT.Sqrt, scale=1.0 / HD, bias=v("eps")).then_inc(s_bank[bank], 1)
                if dve:
                    copied(bank, used + 1)
                    done(e.reciprocal(tmp, tmp), s + "hrs")
                    need(s + "hrs")
                    done(e.scalar_tensor_tensor(out, x, gain, tmp, ALU.mult, ALU.mult), s + "hn")

            def turn_tile(s, bank, used, src, ready):
                if pe:
                    ready()
                    e.wait_ge(s_bank[bank], used + 1)
                    for i in range(NT):
                        mm = e.transpose(ps[bank][:, P * i:P * i + P], src(i), ident)
                    done(mm, s + "tt")

            def by_block(ap):
                return ap.rearrange("p (i f) -> p i f", i=NT)

            if dve:
                need(f"M0{2 * KD - 2}mod", N_FF - 1)
            norm_mod("KV", 2, (96, 104), v("kv_norm_g", 0, 8))
            last("KV", KD - 1)
            u0, b = U[0], list(BK)
            with loop(KD // 2, "pe", "act", "dve") as it:
                for q in range(2):
                    unit_pe(u0, it, q, [(q, b[q] + 2 * it, *FULL, (xh, xl))])
                for q in range(2):
                    kt = bC[:, 2 * it + q, :] if L.name in ("pe", "act", "dve") else None
                    if act:
                        unit_read(u0, it, q)
                    if act or dve:
                        split(u0 + 2, it, q)
                    if act:
                        need(f"K{q}hn", it - 1)
                        apart()
                    copy_out(q, b[q] + 2 * it, kt)
                    head_norm(f"K{q}", q, b[q] + 2 * it, kt, bS[:, q, :], v("k_g"), kt)
            U[0] += KD
            for q in range(2):
                BK[q] += KD
            vtok = bT[:, 0:8, :].rearrange("p a b -> p (a b)").rearrange("p (i f) -> p i f", i=NT)
            u0, b = U[0], list(BK)
            with loop(KD // 2, "pe", "act", "dve") as it:
                for q in range(2):
                    unit_pe(u0, it, q, [(q, b[q] + 2 * it, *FULL, (xh, xl))])
                for q in range(2):
                    if act:
                        unit_read(u0, it, q)
                    if act or dve:
                        split(u0 + 2, it, q)
                    if act:
                        need(f"V{q}tt", it - 1)
                        if q == 0:
                            need("K1hn", KD // 2 - 1)
                    copy_out(q, b[q] + 2 * it, bS[:, q, :])
                    turn_tile(f"V{q}", q, b[q] + 2 * it + 1, lambda i: bS[:, q, P * i:P * i + P],
                              lambda: None)
                    if dve:
                        need(f"V{q}tt")
                        if q == 0:
                            need(f"KVlo{KD - 1}")
                        e.tensor_copy(vtok[:, :, bass.ds(2 * P * it + P * q, P)], by_block(ps[q][:]))\
                         .then_inc(s_bank[q], 1)
            U[0] += KD
            for q in range(2):
                BK[q] += KD

            bDk = lambda k: bD[:, k, :]
            mod_gain("Q", 3, 56, v("norm1_g", 8, 8))
            norm("Q", hk, KD, D, lambda k: gs[:, 3, k:k + 1], lambda k: mod[:, 48 + k:49 + k], xh, xl, [], bDk,
                 bT[:, 9, :], fresh=False)
            last("Q", KD - 1)
            u0, b = U[0], list(BK)
            if act:
                need("V1tt", KD // 2 - 1)
                need(f"Qlo{KD - 1}")
            if dve:
                need(f"Qlo{KD - 1}")
            if pe:
                e.wait_ge(s_bank[0], b[0] + 1)
                e.wait_ge(s_bank[1], b[1] + 1)
            with loop(KD // 2, "pe", "act", "dve", "pool") as it:
                if act:
                    e.wait_ge(s_sread, NX[0] + 16 * it + 2)
                    for n in range(4):
                        e.dma_start(bS[:, n, :], io["attn_bias"][4 * it + n]).then_inc(s_bias, 16)
                for u in range(2):
                    j = 2 * it + u if L.name != "sp" else 0
                    used = b[u] + 3 * it if L.name != "sp" else 0
                    qt, kt = bC[:, 8 + u, :], bC[:, 10, :]
                    unit_pe(u0, it, u, [(u, used, *FULL, (xh, xl))])
                    if act:
                        unit_read(u0, it, u)
                    if act or dve:
                        split(u0 + 2, it, u)
                    if act:
                        e.wait_ge(s_score, NX[0] + 16 * it + (8 * u + 1))
                    copy_out(u, used, qt)
                    head_norm(f"Q{u}", u, used, qt, scratch, v("q_g"), qt)
                    if dve:
                        e.wait_ge(s_score, NX[0] + 16 * it + (8 * u + 1))
                        done(e.tensor_copy(kt, bC[:, j, :]), f"Q{u}k")
                    if pe:
                        need(f"Q{u}k")
                    steps = []
                    for g in range(2):
                        for i in range(NT):
                            nk, r = P * (i + 1), slice(HD * g, HD * g + HD)
                            steps.append(dict(
                                q=[qt[r, P * i:P * i + P]], k=[kt[r, 0:nk]], nk=nk, scale=HD ** -0.5,
                                bias=bS[:, 2 * u + g, T - nk:T], dv=HD, o=o_tok[:, i, HD * g:HD * g + HD],
                                v=[vtok[:, m, bass.ds(P * j + HD * g, HD)] for m in range(i + 1)]))
                    if dve:
                        e.wait_ge(s_bias, 64 * it + 64)
                        need(f"Q{1 - u}tt", it - (u == 0))
                    attend(steps, it, u, 2)

                    def ready():
                        e.wait_ge(s_o, NS[0] + 16 * it + (8 * u + 8 + 2))
                    turn_tile(f"Q{u}", u, used + 2, lambda i: o_tok[:, i, :], ready)
                    if act:
                        need(f"Q{u}tt")
                        need(f"Q{1 - u}olo", it - (u == 0))
                        copy_out(u, used + 2, o_feat)
                        copied(u, used + 2)
                        apart()
                        done(e.activation(bh[:, j, :], o_feat, ACT.Copy), f"Q{u}ohi")
                    if pool:
                        need(f"Q{u}ohi")
                        done(e.tensor_tensor(bl[:, j, :], o_feat, bh[:, j, :].bitcast(F32), ALU.subtract), f"Q{u}olo")
            U[0] += KD
            for q in range(2):
                BK[q] += 3 * KD // 2
            NX[0] += 64
            NS[0] += 64
            NB[0] += 16

            def residual(s, gcol):
                u0, b = U[0], list(BK)
                with loop(KD // 2, "pe", "act", "dve") as it:
                    for q in range(2):
                        unit_pe(u0, it, q, [(q, b[q] + it, *FULL, (bh, bl))])
                        if act:
                            unit_read(u0, it, q)
                        if dve:
                            unit_read(u0, it, q)
                        split(u0 + 2, it, q)
                        if dve:
                            e.scalar_tensor_tensor(h[:, 2 * it + q, :], ps[q][:], mod[:, bass.ds(2 * it + (gcol + q), 1)],
                                                   h[:, 2 * it + q, :], ALU.mult, ALU.add).then_inc(s_bank[q], 1)
                U[0] += KD
                for q in range(2):
                    BK[q] += KD // 2

            if pe:
                need("Q1olo", KD // 2 - 1)
            residual("AO", 64)
            norm_mod("M1n", 4, (72, 80), v("norm2_g", 8, 8), [("Q1olo", KD // 2 - 1)])
            mlp("M1", 88, None)

            R = slice(ROPE0, MLA_QK)
            cos_t, sin_t, t0, t1 = bA[R, 0, :], bA[R, 1, :], bA[R, 2, :], bA[R, 3, :]
            if act:
                e.wait_ge(s_ada, 16 * (N_ADA - ADA_FIRST + 1))
                e.dma_start(t0.bitcast(I32), io["pos"]).then_inc(s_aux, 16)
            if dve:
                e.wait_ge(s_aux, 16)
                done(e.tensor_copy(sin_t, t0.bitcast(I32)), "R0")
                need("R0")
                invf = vec[R, VEC["inv_freq"]:VEC["inv_freq"] + 1]
                done(e.tensor_scalar(sin_t, sin_t, invf, None, ALU.mult), "R1")
                need("R1")
                done(e.tensor_scalar(t0.bitcast(I32), sin_t, 1 / (2 * math.pi), None, ALU.mult), "R2")
                need("R2")
                done(e.tensor_copy(t1, t0.bitcast(I32)), "R3")
                prev = "R3"
                for n, part in enumerate(TWO_PI):
                    need(prev)
                    done(e.scalar_tensor_tensor(sin_t, t1, -part, sin_t, ALU.mult, ALU.add), f"R4{n}")
                    prev = f"R4{n}"
                need(prev)
                done(e.tensor_scalar(cos_t, sin_t, math.pi / 2, None, ALU.add), "R5")
                need("R5")
                done(e.tensor_scalar(t0, cos_t, PI_IN, 2 * math.pi, ALU.is_gt, ALU.mult), "R6")
                need("R6")
                done(e.tensor_tensor(cos_t, cos_t, t0, ALU.subtract), "R7")
                need("R7")
                for n, t in enumerate((cos_t, sin_t)):
                    done(e.tensor_scalar(t, t, PI_IN, -PI_IN, ALU.min, ALU.max), f"R8{n}")
            if act:
                need("R81")
                for t in (cos_t, sin_t):
                    done(e.activation(t, t, ACT.Sin), "R9")
            if dve or act or pe:
                need("R9")

            def rotate(s, bank, used, x, out, tmp):
                if pe:
                    e.wait_ge(s_bank[bank], used + 1)
                    done(e.matmul(ps[bank][:], swap, x, start=True, stop=True), s + "rs")
                if dve:
                    need(s + "rs")
                    e.tensor_tensor(tmp[R, :], ps[bank][R, :], sin_t, ALU.mult).then_inc(s_bank[bank], 1)
                    done(e.tensor_tensor(out[R, :], x[R, :], cos_t, ALU.mult), s + "rc")
                    need(s + "rc")
                    done(e.tensor_tensor(out[R, :], out[R, :], tmp[R, :], ALU.add), s + "ro")
                    need(s + "ro")

            def gate_result(s, t, z, th):
                if dve:
                    need(s + "th")
                    done(e.scalar_tensor_tensor(th, th, 1.0, z, ALU.add, ALU.mult), s + "zz")
                    need(s + "zz")
                    done(e.scalar_tensor_tensor(o_feat, th, 0.5, o_feat, ALU.mult, ALU.mult), s + "y0")
                put(s, 0, o_feat, bh[:, t, :], bl[:, t, :])

            for l in range(2):
                lam_init = 0.8 - 0.6 * math.exp(-0.3 * l)
                n = f"L{l}"
                h_ready()
                norm(n + "n", hk, KD, D, lambda k: v("pre_g", 8 * l + k), None, xh, xl,
                     [(f"L{l - 1}end",)] if l else [("R9",)], bTk, bT[:, 9, :])
                if dve:
                    dl = v("da_l", 256 * l, 256).rearrange("p (a d) -> p a d", a=4)
                    for m in range(2):
                        done(e.tensor_tensor(scratch[:, HD * m:HD * m + HD], dl[:, 2 * m, :], dl[:, 2 * m + 1, :], ALU.mult), n + "l0")
                    need(n + "l0")
                    for m in range(2):
                        done(e.tensor_reduce(sm[:, SLN + m:SLN + m + 1], scratch[:, HD * m:HD * m + HD], AX, ALU.add), n + "l1")
                if act:
                    need(n + "l1")
                    done(e.activation(sm[:, SLN:SLN + 2], sm[:, SLN:SLN + 2], ACT.Exp), n + "l2")
                if dve:
                    need(n + "l2")
                    done(e.tensor_tensor(sm[:, SLN + 2:SLN + 3], sm[:, SLN + 1:SLN + 2], sm[:, SLN:SLN + 1], ALU.subtract), n + "l3")
                    need(n + "l3")
                    done(e.tensor_scalar(sm[:, SLN + 2:SLN + 3], sm[:, SLN + 2:SLN + 3], lam_init, None, ALU.subtract), n + "l4")
                    need(n + "l4")
                last(n + "n", KD - 1)
                if act or dve:
                    need(f"{n}nlo{KD - 1}")

                def branch_sum(s, first_branch):
                    u0, b = U[0], list(BK)
                    with loop(2, "pe", "act", "dve", "pool") as it:
                        for r in range(2):
                            for m in range(2):
                                bk = (3 * r + m) % 2
                                unit_pe(u0, 3 * it, 3 * r + m, [(bk, b[bk] + 2 * it + r, *FULL, (xh, xl))])
                            unit_pe(u0, 3 * it, 3 * r + 2,
                                    [(2 + m, b[2 + m] + 2 * it + r, range(4 * m, 4 * m + 4), range(4), (bh, bl))
                                     for m in range(2)])
                            for m in range(2):
                                bk = (3 * r + m) % 2
                                if act:
                                    unit_read(u0, 3 * it, 3 * r + m)
                                if act or dve:
                                    split(u0 + 2, 3 * it, 3 * r + m)
                                if act:
                                    e.wait_ge(s_bank[2 + m], b[2 + m] + 2 * it + r + 1)
                                    done(e.activation(bS[:, m, :], ps[bk][:], ACT.Tanh, scale=0.5), f"{s}th{r}{m}")
                                    need(f"{s}th{r}{m}")
                                    e.sem_inc(s_bank[bk], 1)
                            if act or dve:
                                unit_read(u0, 3 * it, 3 * r + 2)
                                split(u0 + 2, 3 * it, 3 * r + 2)
                            for m in range(2):
                                y = bT[:, 4 * it + (2 * r + m), :] if L.name != "sp" else None
                                if dve:
                                    need(f"{s}th{r}{m}")
                                    if not first_branch:
                                        need(f"{s}add{1 - r}{m}", it - (r == 0))
                                    e.scalar_tensor_tensor(y if first_branch else bS[:, 2 + m, :], bS[:, m, :], 1.0,
                                                           ps[2 + m][:], ALU.add, ALU.mult).then_inc(s_bank[2 + m], 1)
                                if pool and not first_branch:
                                    e.wait_ge(s_bank[2 + m], b[2 + m] + 2 * it + r + 2)
                                    done(e.tensor_tensor(y, y, bS[:, 2 + m, :], ALU.add), f"{s}add{r}{m}")
                    U[0] += 12
                    for q in range(4):
                        BK[q] += 4

                s = n + "D"
                u0, b = U[0], list(BK)
                qt, kt, vt, zt, th, bi, vk = (bC[:, k, :] for k in range(7))
                vk = by_block(vk)
                steps = []
                for i in range(NT):
                    nk = P * (i + 1)
                    steps.append(dict(q=[qt[HD * m:HD * m + HD, P * i:P * i + P] for m in range(2)],
                                      k=[kt[HD * m:HD * m + HD, 0:nk] for m in range(2)], nk=nk, scale=HD ** -0.5,
                                      bias=bi[:, T - nk:T], dv=P, o=o_tok[:, i, :], lam=sm[:, SLN + 2:SLN + 3],
                                      v=[vk[:, m, :] for m in range(i + 1)]))
                with loop(4, "pe", "act", "dve", "pool") as it:
                    c0, c1 = b[0] + 4 * it, b[1] + 2 * it
                    if act:
                        e.wait_ge(s_sread, NX[0] + 8 * it + 2)
                        e.dma_start(bi, io["da_bias"][it]).then_inc(s_bias, 16)
                    for q, (bk, used) in enumerate([(0, c0), (1, c1), (0, c0 + 1), (1, c1 + 1)]):
                        unit_pe(u0, 2 * it, q, [(bk, used, *FULL, (xh, xl))])
                    for q, (bk, used, dst) in enumerate([(0, c0, qt), (1, c1, kt), (0, c0 + 1, vt), (1, c1 + 1, zt)]):
                        if act:
                            unit_read(u0, 2 * it, q)
                        if act or dve:
                            split(u0 + 2, 2 * it, q)
                        if act:
                            if q == 3:
                                need(s + "zz", it - 1)
                            if q == 2:
                                need(s + "tt0tt", it - 1)
                            if q == 0:
                                e.wait_ge(s_score, NX[0] + 8 * it + 1)
                        copy_out(bk, used, dst)
                    if act:
                        copied(1, c1 + 1)
                        done(e.activation(th, zt, ACT.Tanh, scale=0.5), s + "th")
                    turn_tile(s + "tt0", 0, c0 + 2, lambda i: vt[:, P * i:P * i + P], lambda: None)
                    if dve:
                        need(s + "tt0tt")
                        e.tensor_copy(vk, by_block(ps[0][:])).then_inc(s_bank[0], 1)
                    if pe:
                        copied(0, c0 + 2)
                        copied(1, c1 + 1)
                    if dve:
                        e.wait_ge(s_bias, 16 * (NB[0] + 1) + 16 * it)
                        need(s + "tt1tt", it - 1)
                    attend(steps, it)
                    if act:
                        e.wait_ge(s_o, NS[0] + 4 * it + (4 + 2))
                        for i in range(NT):
                            done(e.activation(bD[:, 0, P * i:P * i + P], o_tok[:, i, :], ACT.Square,
                                              accum_out=sm[:, SSQ + i:SSQ + i + 1]), s + "ssq")
                        need(s + "ssq")
                        done(e.activation(sm[:, SSQ:SSQ + NT], sm[:, SSQ:SSQ + NT], ACT.Sqrt, scale=1.0 / P, bias=v("eps")), s + "srt")
                    if dve:
                        need(s + "srt")
                        done(e.reciprocal(sm[:, SSQ:SSQ + NT], sm[:, SSQ:SSQ + NT]), s + "srs")
                        need(s + "srs")
                        for i in range(NT):
                            done(e.tensor_scalar(o_tok[:, i, :], o_tok[:, i, :], sm[:, SSQ + i:SSQ + i + 1], None, ALU.mult), s + "sub")
                    turn_tile(s + "tt1", 0, c0 + 3, lambda i: o_tok[:, i, :], lambda: need(s + "sub"))
                    if dve:
                        need(s + "tt1tt")
                        need(s + "lo0", it - 1)
                        e.tensor_scalar(o_feat, ps[0][:], v("subln", l), 1.0 - lam_init, ALU.mult, ALU.mult)\
                         .then_inc(s_bank[0], 1)
                        copied(0, c0 + 3)
                    gate_result(s, it, zt, th)
                attended(steps, 4)
                U[0] += 16
                BK[0] += 16
                BK[1] += 8
                NB[0] += 4
                if pe:
                    need(s + "lo0", 3)
                branch_sum(n + "E", True)

                s = n + "B"
                u0, b = U[0], list(BK)
                for q in range(4):
                    unit_pe(u0, 0, q, [(q % 2, b[q % 2] + q // 2, *FULL, (xh, xl))])
                    if act:
                        unit_read(u0, 0, q)
                        if q == 0:
                            e.wait_ge(s_bank[2], b[2] + 1)
                            e.wait_ge(s_bank[3], b[3] + 1)
                    split(u0 + 2, 0, q)
                    copy_out(q % 2, b[q % 2] + q // 2, bS[:, q, :])
                U[0] += 4
                for q in range(2):
                    BK[q] += 2
                if act or dve or pe:
                    copied(0, BK[0] - 1)
                    copied(1, BK[1] - 1)
                norm(s + "q", lambda k: bS[:, k, :], 2, 2 * P, lambda k: v("mq_g", 2 * l + k), None,
                     bh[:, 8:10, :], bl[:, 8:10, :], [], lambda k: bC[:, k, :], bC[:, 2, :])
                norm(s + "k", lambda k: bS[:, 2, :], 1, P, lambda k: v("mkv_g", l), None,
                     bh[:, 10:11, :], bl[:, 10:11, :], [(s + "qlo1",)], lambda k: bC[:, 3, :], bC[:, 4, :])
                ks = [bA[:, 2, :], bA[:, 3, :]]
                rotate(s + "r", 0, BK[0], bS[:, 3, :], ks[0], scratch)
                if dve:
                    need(s + "rro")
                    done(e.tensor_copy(ks[1][R, :], ks[0][R, :]), s + "rk")
                BK[0] += 1
                if act:
                    need(s + "rk")
                    e.dma_start(bC[:, 7, :], io["mask"]).then_inc(s_bias, 16)
                last(s + "k", 0)
                NB[0] += 1
                u0, b = U[0], list(BK)
                qt, kv = [bC[:, 0, :], bC[:, 2, :]], [bC[:, 1, :], bC[:, 3, :]]
                zt, th, vk = bC[:, 4, :], bC[:, 5, :], by_block(bC[:, 6, :])
                qk_hl, kv_hl = (bh[:, 8:10, :], bl[:, 8:10, :]), (bh[:, 10:11, :], bl[:, 10:11, :])
                steps = []
                for g in range(2):
                    for i in range(NT):
                        nk = P * (i + 1)
                        steps.append(dict(q=[qt[g][0:MLA_QK, P * i:P * i + P]], k=[ks[g][0:MLA_QK, 0:nk]], nk=nk,
                                          scale=MLA_QK ** -0.5, bias=bC[:, 7, T - nk:T], dv=HD,
                                          o=o_tok[:, i, HD * g:HD * g + HD],
                                          v=[vk[:, m, HD * g:HD * g + HD] for m in range(i + 1)]))
                if act or dve:
                    need(s + "klo0")
                if dve:
                    e.wait_ge(s_bias, 16 * NB[0])
                with loop(4, "pe", "act", "dve", "pool") as it:
                    c0, c1 = b[0] + 5 * it, b[1] + 5 * it
                    if pe:
                        p, k = place(u0, it, 0)
                        e.wait_ge(s_lo, 2 * k + p + 1)
                        for g in range(2):
                            e.wait_ge(s_bank[0], c0 + (g + 1))
                            for m in range(2):
                                mm = mm3(ps[0][:], p, 2 * g + m, qk_hl[0][:, m, :], qk_hl[1][:, m, :], m == 0, m == 1)
                            done(mm, f"{s}q{g}")
                            e.wait_ge(s_bank[1], c1 + (g + 1))
                            mm = mm3(ps[1][:], p, 4 + g, kv_hl[0][:, 0, :], kv_hl[1][:, 0, :], True, True)
                            if g == 0:
                                done(mm, f"{s}k{g}")
                        mm.then_inc(s_unit, 1)
                    if act:
                        e.wait_ge(s_score, NX[0] + 8 * it + 1)
                        need(s + "t1tt", it - 1)
                        need(s + "kc1", it - 1)
                        for g in range(2):
                            need(f"{s}q{g}")
                            copy_out(0, c0 + g, qt[g])
                            if g == 0:
                                need(f"{s}k{g}")
                            else:
                                unit_read(u0, it, 0)
                            copy_out(1, c1 + g, kv[g])
                    if act or dve:
                        split(u0 + 2, it, 0)
                    unit_pe(u0, it, 1, [(1, c1 + 2, *FULL, (xh, xl))])
                    if act:
                        unit_read(u0, it, 1)
                    if act or dve:
                        split(u0 + 2, it, 1)
                    if act:
                        need(s + "zz", it - 1)
                    copy_out(1, c1 + 2, zt)
                    if act:
                        copied(1, c1 + 2)
                        done(e.activation(th, zt, ACT.Tanh, scale=0.5), s + "th")
                    if dve:
                        copied(0, c0 + 1)
                        copied(1, c1 + 1)
                    if pe:
                        copied(0, c0 + 1)
                        copied(1, c1 + 1)
                    for g in range(2):
                        rotate(f"{s}{g}", 0, c0 + 2 + g, qt[g], qt[g], scratch)
                        turn_tile(f"{s}t{g}", 1, c1 + 3 + g, lambda i: kv[g][:, P * i:P * i + P], lambda: None)
                        if dve:
                            done(e.tensor_copy(ks[g][0:HD, :], kv[g][0:HD, :]), f"{s}kc{g}")
                            need(f"{s}t{g}tt")
                            e.tensor_copy(vk[:, :, HD * g:HD * g + HD], by_block(ps[1][:])[:, :, HD:P])\
                             .then_inc(s_bank[1], 1)
                    if pe:
                        need(f"{s}1ro")
                        copied(1, c1 + 4)
                    if dve:
                        need(s + "ot", it - 1)
                    attend(steps, it)
                    if pe:
                        e.wait_ge(s_o, NS[0] + 8 * it + (8 + 2))
                        e.wait_ge(s_bank[0], c0 + 5)
                        for i in range(NT):
                            mm = e.transpose(ps[0][:, P * i:P * i + P], o_tok[:, i, :], ident)
                        done(mm, s + "ot")
                    if dve:
                        need(s + "ot")
                        need(s + "lo0", it - 1)
                        e.tensor_copy(o_feat, ps[0][:]).then_inc(s_bank[0], 1)
                        copied(0, c0 + 4)
                    gate_result(s, it, zt, th)
                attended(steps, 4)
                U[0] += 8
                BK[0] += 20
                BK[1] += 20
                if pe:
                    need(s + "lo0", 3)
                branch_sum(n + "F", False)

                s = n + "S"
                u0, b = U[0], list(BK)
                qt, kt, vt, zt, th = (bC[:, k, :] for k in range(5))
                vk = by_block(bC[:, 6, :])
                if act:
                    e.wait_ge(s_bank[1], b[1] + 1)
                for q, dst in enumerate((kt, vt)):
                    unit_pe(u0, 0, q, [(q, b[q], *FULL, (xh, xl))])
                    if act:
                        unit_read(u0, 0, q)
                    split(u0 + 2, 0, q)
                    copy_out(q, b[q], dst)
                turn_tile(s + "v", 1, b[1] + 1, lambda i: vt[:, P * i:P * i + P], lambda: None)
                if dve:
                    need(s + "vtt")
                    e.tensor_copy(vk, by_block(ps[1][:])).then_inc(s_bank[1], 1)
                U[0] += 2
                BK[0] += 1
                BK[1] += 2
                if pe:
                    e.wait_ge(s_bank[0], BK[0] + 1)
                    e.wait_ge(s_bank[1], BK[1] + 1)
                u0, b = U[0], list(BK)
                bi = bC[:, 5, :].rearrange("p (g k) -> p g k", g=2)
                with loop(4, "pe", "act", "dve", "pool") as it:
                    steps = []
                    for g in range(2):
                        r = slice(HD * g, HD * g + HD)
                        for i in range(NT):
                            k0 = P * max(i - 1, 0)
                            nk = P * (i + 1) - k0
                            steps.append(dict(q=[qt[r, P * i:P * i + P]], k=[kt[r, k0:k0 + nk]], nk=nk, scale=HD ** -0.5,
                                              bias=bi[:, g, 2 * P - nk:2 * P], dv=HD, o=o_tok[:, i, r],
                                              sink=vdyn("sinks", 8 * l + 4 * g + it) if act or dve else 0,
                                              v=[vk[:, m, r] for m in range(k0 // P, i + 1)]))
                    c0, c1 = b[0] + 2 * it, b[1] + it
                    if act:
                        e.wait_ge(s_sread, NX[0] + 8 * it + 2)
                        for g in range(2):
                            e.dma_start(bi[:, g, :], io["sw_bias"][it + 4 * g]).then_inc(s_bias, 16)
                    for q, (bk, used, dst) in enumerate([(0, c0, qt), (1, c1, zt)]):
                        unit_pe(u0, it, q, [(bk, used, *FULL, (xh, xl))])
                        if act:
                            unit_read(u0, it, q)
                        if act or dve:
                            split(u0 + 2, it, q)
                        if act:
                            if q == 0:
                                e.wait_ge(s_score, NX[0] + 8 * it + 1)
                            else:
                                need(s + "zz", it - 1)
                        copy_out(bk, used, dst)
                    if act:
                        copied(1, c1)
                        done(e.activation(th, zt, ACT.Tanh, scale=0.5), s + "th")
                    if pe:
                        copied(0, c0)
                    if dve:
                        copied(1, c1)
                        e.wait_ge(s_bias, 16 * (NB[0] + 2) + 32 * it)
                        need(s + "ot", it - 1)
                    attend(steps, it)
                    if pe:
                        e.wait_ge(s_o, NS[0] + 8 * it + (8 + 2))
                        e.wait_ge(s_bank[0], c0 + 2)
                        for i in range(NT):
                            mm = e.transpose(ps[0][:, P * i:P * i + P], o_tok[:, i, :], ident)
                        done(mm, s + "ot")
                    if dve:
                        need(s + "ot")
                        need(s + "lo0", it - 1)
                        e.tensor_copy(o_feat, ps[0][:]).then_inc(s_bank[0], 1)
                        copied(0, c0 + 1)
                    gate_result(s, it, zt, th)
                attended(steps, 4)
                U[0] += 8
                BK[0] += 8
                BK[1] += 4
                NB[0] += 8
                if pe:
                    need(s + "lo0", 3)
                branch_sum(n + "H", False)

                s = n + "O"
                if act:
                    e.wait_ge(s_unit, U[0])
                    NA[0] += 1
                    e.dma_start(bD[:, 0:2, :], io["ple"][l]).then_inc(s_aux, 16)
                for k in range(KD):
                    if dve:
                        need(f"{n}Hadd{1}{1}", 1)
                        done(e.tensor_scalar(bT[:, k, :], bT[:, k, :], 0.5, None, ALU.mult), f"{s}y{k}")
                    put(s, k, bT[:, k, :], bh[:, k, :], bl[:, k, :])
                u0, b = U[0], list(BK)
                last(s, KD - 1)
                if act:
                    need(n + "Szz", 3)
                with loop(KD // 2, "pe", "act", "dve") as it:
                    for q in range(2):
                        unit_pe(u0, it, q, [(q, b[q] + it, *FULL, (bh, bl))])
                        if act:
                            unit_read(u0, it, q)
                        if act or dve:
                            split(u0 + 2, it, q)
                        if act:
                            e.activation(bC[:, 2 * it + q, :], ps[q][:], ACT.Copy).then_inc(s_bank[q], 1)
                U[0] += KD
                for q in range(2):
                    BK[q] += KD // 2
                if act or dve:
                    e.wait_ge(s_bank[0], BK[0] + 1)
                    e.wait_ge(s_bank[1], BK[1] + 1)
                if dve:
                    e.wait_ge(s_aux, 32 + 16 * l)
                    for k in range(2):
                        done(e.tensor_scalar(bD[:, k, :], bD[:, k, :], 1.0, None, ALU.mult), f"{n}py{k}")
                for k in range(2):
                    put(n + "p", k, bD[:, k, :], bh[:, 8 + k, :], bl[:, 8 + k, :])
                stats(s + "z", lambda k: bC[:, k, :], KD, D, lambda k: bD[:, 2 + k, :], bT[:, 9, :], [])
                if dve:
                    need(s + "zrstd")
                    for k in range(KD):
                        done(e.tensor_tensor(bC[:, k, :], bC[:, k, :], bT[:, 9, :], ALU.mult), f"{s}n{k}")
                        need(f"{s}n{k}")
                        done(e.scalar_tensor_tensor(h[:, k, :], bC[:, k, :], v("post_g", 8 * l + k), h[:, k, :],
                                                    ALU.mult, ALU.add), f"{n}xy{k}")
                for k in range(KD):
                    put(n + "x", k, h[:, k, :], xh[:, k, :], xl[:, k, :])

                u0, b = U[0], list(BK)
                last(n + "p", 1)
                if act:
                    need(f"{s}lo{KD - 1}")
                for q in range(2):
                    if pe:
                        p, k = place(u0, 0, q)
                        e.wait_ge(s_lo, 2 * k + p + 1)
                        for m in range(4):
                            e.wait_ge(s_bank[m], b[m] + q + 1)
                            for kt in range(2):
                                mm = mm3(ps[m][:], p, 2 * m + kt, bh[:, 8 + kt, :], bl[:, 8 + kt, :], kt == 0, kt == 1)
                            if m < 3:
                                done(mm, f"{n}pp{q}{m}")
                        mm.then_inc(s_unit, 1)
                    if act:
                        for m in range(4):
                            if m < 3:
                                need(f"{n}pp{q}{m}")
                            else:
                                unit_read(u0, 0, q)
                            e.activation(bT[:, 4 * q + m, :], ps[m][:], ACT.Copy).then_inc(s_bank[m], 1)
                    split(u0 + 2, 0, q)
                U[0] += 2
                for m in range(4):
                    BK[m] += 2
                if dve:
                    for m in range(4):
                        e.wait_ge(s_bank[m], BK[m] + 1)
                last(n + "x", KD - 1)
                if dve:
                    need(f"{n}xlo{KD - 1}")
                u0, b = U[0], list(BK)
                s = n + "P"
                with loop(KD // 2, "pe", "act", "dve") as it:
                    for q in range(2):
                        unit_pe(u0, it, q, [(q, b[q] + it, *FULL, (xh, xl))])
                        if act:
                            unit_read(u0, it, q)
                        if act or dve:
                            split(u0 + 2, it, q)
                        if act:
                            need(f"{s}m{q}", it - 1)
                            e.activation(bS[:, q, :], ps[q][:], ACT.Tanh, scale=0.5).then_inc(s_bank[q], 1)
                        if dve:
                            copied(q, b[q] + it)
                            done(e.scalar_tensor_tensor(bS[:, 2 + q, :], bS[:, q, :], 1.0, bT[:, 2 * it + q, :], ALU.add, ALU.mult), f"{s}m{q}")
                            need(f"{s}m{q}")
                            done(e.scalar_tensor_tensor(h[:, 2 * it + q, :], bS[:, 2 + q, :], 0.5, h[:, 2 * it + q, :], ALU.mult, ALU.add), f"{s}h{q}")
                U[0] += KD
                for q in range(2):
                    BK[q] += KD // 2
                if dve or act:
                    need(f"{s}h1", KD // 2 - 1)
                if dve:
                    done(e.tensor_copy(sm[:, 63:64], sm[:, 0:1]), f"L{l}end")
            if sp:
                need("L1end")
                e.dma_start(io["out"], h[:]).then_inc(s_out, 16)
                e.wait_ge(s_out, 16)
                for p in range(2):
                    e.wait_ge(s_raw[p], 16 * (io["units"] // 2))
            assert U[0] + 2 == io["units"], U[0]

        for eng, name in ((block.sync, "sp"), (block.tensor, "pe"), (block.scalar, "act"),
                          (block.vector, "dve"), (block.gpsimd, "pool")):
            @eng
            def _(e, name=name):
                program(Lane(name, e, sems[name], plan))


@contextmanager
def _skip():
    yield 0


def _stream(a):
    units, blocks = [], []

    def block(w=None, r=0, cols=None):
        b = np.zeros((P, P), np.float32)
        if w is not None:
            part = w[r:r + P, cols]
            b[:part.shape[0], :part.shape[1]] = part
        blocks.append(b)
        if len(blocks) == UB:
            units.append(np.stack(blocks, 1))
            blocks.clear()

    def cols(n, width=P):
        return slice(n, n + width)

    def column(w, c, k0=0, n=KD):
        for k in range(n):
            block(w, P * (k0 + k), c)

    w_in = a["lru_w_in"][0]
    for j in range(KW):
        column(w_in, cols(W + P * j))
        column(w_in, cols(P * j))
    gates = []
    for name in ("lru_gate_a_w", "lru_gate_x_w"):
        full = np.zeros((W, W), np.float32)
        for n, blk in enumerate(a[name][0]):
            full[LRU_BLK * n:LRU_BLK * (n + 1), LRU_BLK * n:LRU_BLK * (n + 1)] = blk
        gates.append(full)
    for j in range(KW):
        for full in gates:
            for k in (j - 1, j, j + 1):
                block(full if 0 <= k < KW else None, P * k, cols(P * j))
        block()
        block()
    for n in range(KD):
        column(a["lru_w_out"][0], cols(P * n), 0, KW)

    def mlp(l):
        for c in range(N_FF):
            for n in range(KD):
                column(a["mlp_w1"][l], cols(D * c + P * n))
            for n in range(KD):
                column(a["mlp_w2"][l], cols(P * n), KD * c)

    mlp(0)
    for n in range(2 * KD):
        column(a["kv_w"], cols(P * n))
    for w in (a["attn_w_q"][0], a["attn_w_o"][0]):
        for n in range(KD):
            column(w, cols(P * n))
    mlp(1)
    heads = [np.r_[HD * t:HD * (t + 1), HD * (t + 4):HD * (t + 5)] for t in range(4)]
    for l in range(2):
        w = a["w_in_2"][l]
        o = IN_OFF

        def branch(n, wb, rows):
            wb = wb[rows]
            for m in range(0, KD, 2):
                for g in range(2):
                    column(w, cols(o["g"] + D * n + P * (m + g)))
                for g in range(2):
                    column(wb, cols(P * (m + g)), 0, 4)

        for t in range(4):
            for name in ("aq", "ak", "av", "az"):
                column(w, cols(o[name] + P * t))
        branch(0, a["w_br_a_2"][l], slice(None))
        for c in (cols(o["bq"]), cols(o["bq"] + P), cols(o["bkv"]), cols(o["bkr"] - ROPE0, MLA_QK)):
            column(w, c)
        for t in range(4):
            for g in range(2):
                for k in range(2):
                    block(a["mla_w_qb_2"][l], P * k, cols(MLA_QK * (2 * t + g), MLA_QK))
            for g in range(2):
                block(a["mla_w_kvb_2"][l], 0, cols(P * (2 * t + g)))
            block()
            block()
            column(w, cols(o["bz"] + P * t))
        branch(1, a["w_br_b_2"][l], slice(None))
        column(w, cols(o["ck"]))
        column(w, cols(o["cv"]))
        for t in range(4):
            column(w, o["cq"] + heads[t])
            column(w, o["cz"] + heads[t])
        branch(2, a["w_br_c_2"][l], np.concatenate(heads))
        for n in range(KD):
            column(a["w_out_2"][l], cols(P * n))
        for n in range(KD):
            column(a["w_ple_proj_2"][l], cols(P * n), 0, 2)
        for n in range(KD):
            column(a["w_ple_gate_2"][l], cols(P * n))
    assert not blocks
    units += [np.zeros((P, UB, P), np.float32)] * 2
    return np.stack(units)


def _features(x):
    return np.ascontiguousarray(np.asarray(x).reshape(-1, P).T)


def _vectors(a):
    def rows(x):
        return np.broadcast_to(np.asarray(x).reshape(1, -1), (P, np.asarray(x).size))

    freq = np.zeros((P, 1), np.float32)
    half = (MLA_QK - ROPE0) // 2
    f = (np.float32(10000.0) ** (-np.arange(half, dtype=np.float32) / half)).astype(np.float32)
    freq[ROPE0:MLA_QK, 0] = np.concatenate([f, f])
    two = lambda x: np.concatenate([x, x])
    parts = dict(
        c=_features(a["c"]), ada_b=np.concatenate([_features(a["ada_b"]), _features(a["kv_ada_b"])], 1),
        norm1_g=_features(a["norm1_g"]), norm2_g=_features(a["norm2_g"]), kv_norm_g=_features(a["kv_norm_g"]),
        conv_w=_features(a["lru_conv_w"]), conv_b=_features(a["lru_conv_b"]), ga_b=_features(a["lru_gate_a_b"]),
        gx_b=_features(a["lru_gate_x_b"]), lam=_features(a["lru_lambda"]), k_g=_features(two(a["k_norm_g"])),
        q_g=_features(two(a["q_norm_g"][0])), pre_g=_features(a["norm_pre_2"]), post_g=_features(a["norm_post_2"]),
        mq_g=_features(a["mla_q_norm_2"]), mkv_g=_features(a["mla_kv_norm_2"]), subln=_features(a["da_subln_2"]),
        sinks=rows(a["sw_sinks_2"]), da_l=rows(a["da_lambda_2"]), inv_freq=freq,
        eps=np.full((P, 1), EPS, np.float32))
    return np.ascontiguousarray(np.concatenate([parts[k] for k in VEC], 1))


def _bucket(rel):
    n = np.maximum(rel, 0)
    nf = np.maximum(n, 1).astype(np.float32)
    large = 16 + (np.log(nf / np.float32(16)) / np.float32(math.log(128 / 16)) * np.float32(16)).astype(np.int32)
    return np.where(n < 16, n, np.minimum(large, 31))


def _biases(a):
    p, j = np.arange(P)[:, None], np.arange(T)[None, :]
    rel = p - (j - (T - P))
    chunk = a["rel_bias"][0][:, np.clip(rel, -128, 128) + 128]
    chunk = np.where((p < 64) & (j >= T - 64), np.float32(NEG), chunk)
    table = a["rel_bias_2"]
    da = np.where(rel < 0, np.float32(NEG), np.moveaxis(table[_bucket(rel)][..., :4], -1, 0))
    mask = np.where(rel < 0, np.float32(NEG), np.float32(0)).astype(np.float32)
    rel = P + p - np.arange(2 * P)[None, :]
    sw = np.where((rel < 0) | (rel >= 128), np.float32(NEG), np.moveaxis(table[_bucket(rel)][..., 4:], -1, 0))
    return [np.ascontiguousarray(x.astype(np.float32)) for x in (chunk, da, mask, sw)]


def kernel(**inputs):
    import concourse.bacc as bacc
    from concourse.bass_utils import run_bass_kernel_spmd

    a = {k: np.asarray(x) for k, x in inputs.items()}
    tiles = lambda x: np.ascontiguousarray(x.T.reshape(-1, P, T).transpose(1, 0, 2))
    stream = _stream(a)
    ada = np.concatenate([a["ada_w"][0], a["ada_w"][1], a["kv_ada_w"], np.zeros((D, 256), np.float32)], 1)
    ada = np.ascontiguousarray(ada.reshape(KD, P, N_ADA + 1, 256).transpose(2, 1, 0, 3))
    cst = np.zeros((P, 4, P), np.float32)
    cst[:, 0] = np.eye(P)
    cst[:, 1] = 1.0
    cst[:HD, 2, :HD] = 1.0
    cst[HD:, 2, HD:] = 1.0
    for m in range(16):
        cst[ROPE0 + 16 + m, 3, ROPE0 + m] = -1.0
        cst[ROPE0 + m, 3, ROPE0 + 16 + m] = 1.0
    chunk, da, mask, sw = _biases(a)
    ins = dict(w=stream, ada=ada, vec=_vectors(a), cst=cst, x=tiles(a["x"][0]),
               ple=np.stack([tiles(a["p_2"][l, 0]) for l in range(2)]),
               pos=np.ascontiguousarray(np.broadcast_to(a["positions_2"].astype(np.int32), (MLA_QK - ROPE0, T))),
               attn_bias=chunk, da_bias=da, mask=mask, sw_bias=sw)

    counted = {"events": {}, "per_iteration": {}}
    for _ in range(2):
        nc = bacc.Bacc("TRN2", target_bir_lowering=False, num_devices=1)
        io = {k: nc.dram_tensor(f"in_{k}", x.shape, mybir.dt.from_np(x.dtype), kind="ExternalInput").ap()
              for k, x in ins.items()}
        io["out"] = nc.dram_tensor("out", (P, KD, T), F32, kind="ExternalOutput").ap()
        io["units"] = stream.shape[0]
        plan = {"events": {}, "per_iteration": {}, "n": 0}
        build(nc, io, plan, counted)
        counted = plan
    r = run_bass_kernel_spmd(nc, [{f"in_{k}": x for k, x in ins.items()}], core_ids=[0])
    out = r.results[0]["out"]
    return np.ascontiguousarray(out.transpose(1, 0, 2).reshape(D, T).T)[None]
```

```python
from contextlib import ExitStack, contextmanager
import math

import numpy as np

import concourse.bass as bass
from concourse import mybir

F32 = mybir.dt.float32
F32R = mybir.dt.float32r
I32 = mybir.dt.int32
ALU = mybir.AluOpType
ACT = mybir.ActivationFunctionType
AX = mybir.AxisListType.X

P = 128
T = 512
D = 1024
KD = D // P
NT = T // P
W = 1408
KW = W // P
LRU_BLK = 88
UB = 8
NEG = -1e30
EPS = 1e-6
LRU_C = 8.0
HD = 64
MLA_QK = 96
ROPE0 = 64
N_FF = 4
IN_OFF = dict(zip("aq ak av az bq bkv bkr bz cq ck cv cz g".split(),
                  np.cumsum([0, 512, 512, 512, 512, 256, 128, 32, 512, 512, 128, 128, 512]).tolist()))
TWO_PI = []
for _bits in (6, 15, 24):
    _part = round((2 * math.pi - sum(TWO_PI)) * 2 ** _bits) / 2 ** _bits
    TWO_PI.append(_part)
TWO_PI.append(2 * math.pi - sum(TWO_PI))
PI_IN = float(np.nextafter(np.float32(math.pi), np.float32(0)))
N_ADA = 56
ADA_FIRST = 8

VEC = {}
_at = 0
for _name, _n in [("c", 8), ("ada_b", 112), ("norm1_g", 16), ("norm2_g", 16), ("kv_norm_g", 8),
                  ("conv_w", 44), ("conv_b", 11), ("ga_b", 11), ("gx_b", 11), ("lam", 11),
                  ("k_g", 1), ("q_g", 1), ("pre_g", 16), ("post_g", 16), ("mq_g", 4), ("mkv_g", 2),
                  ("subln", 2), ("sinks", 16), ("da_l", 512), ("inv_freq", 1), ("eps", 1)]:
    VEC[_name] = _at
    _at += _n
NVEC = _at


def lru_tiles(j):
    first, last = P * j // LRU_BLK, (P * (j + 1) - 1) // LRU_BLK
    return list(range(LRU_BLK * first // P, (LRU_BLK * (last + 1) - 1) // P + 1))


class Lane:

    def __init__(self, name, eng, sem, plan):
        self.name, self.e, self.sem, self.plan = name, eng, sem, plan
        self.total, self.local, self.in_loop, self.i = 0, 0, None, None

    @contextmanager
    def loop(self, n):
        self.in_loop, self.local = f"{self.name}{self.total}_{self.plan['n']}", 0
        self.plan["n"] += 1
        with self.e.Fori(0, n) as i:
            self.i = i
            yield i
        self.plan["per_iteration"][self.in_loop] = self.local
        self.total += n * self.local
        self.in_loop, self.i, self.local = None, None, 0

    def done(self, ins, ev):
        ins.then_inc(self.sem, 1)
        if self.in_loop is None:
            self.total += 1
        else:
            self.local += 1
        self.plan["events"][ev] = (self.name, self.total + self.local, self.in_loop)


def build(nc, io, plan, counted):
    ctx = ExitStack()
    with ctx:
        def sb(name, shape, dt=F32):
            return ctx.enter_context(nc.sbuf_tensor(name, shape, dt))

        def sem(name):
            return ctx.enter_context(nc.semaphore(name))

        h = sb("h", [P, KD, T])
        xh, xl = sb("xh", [P, KD, T], F32R), sb("xl", [P, KD, T], F32R)
        bh, bl = sb("bh", [P, KW, T], F32R), sb("bl", [P, KW, T], F32R)
        bC, bD, bT = sb("bC", [P, KW, T]), sb("bD", [P, KW, T]), sb("bT", [P, KW, T])
        bS = sb("bS", [P, 4, T])
        raw = [sb(f"raw{p}", [P, UB, P]) for p in range(2)]
        wh = [sb(f"wh{p}", [P, UB, P], F32R) for p in range(2)]
        wl = [sb(f"wl{p}", [P, UB, P], F32R) for p in range(2)]
        bA = sb("bA", [P, 4, T])
        acc = sb("acc", [P, 3, 256])
        vec = sb("vec", [P, NVEC])
        cst = sb("cst", [P, 4, P])
        mod = sb("mod", [P, 112])
        gs = sb("gs", [P, 5, KD])
        sm = sb("sm", [P, 64])
        ps = [ctx.enter_context(nc.psum_tensor(f"ps{b}", [P, T], F32)) for b in range(8)]
        ident, ones, ones64, swap = (cst[:, k, :] for k in range(4))
        SC, SLAM, SBA, SBX, SNM, SRS, SES, SRI, SLN, SSQ = 0, 8, 19, 30, 41, 45, 49, 53, 57, 60

        s_raw = [sem(f"s_raw{p}") for p in range(2)]
        s_hi, s_lo = sem("s_hi"), sem("s_lo")
        s_unit = sem("s_unit")
        s_bank = [sem(f"s_bank{b}") for b in range(4)]
        s_par = sem("s_par")
        s_x = sem("s_x")
        s_a0 = [sem(f"s_a0{k}") for k in range(ADA_FIRST)]
        s_ada = sem("s_ada")
        s_acc = sem("s_acc")
        s_col = sem("s_col")
        s_mod = sem("s_mod")
        s_aux = sem("s_aux")
        s_bias = sem("s_bias")
        s_out = sem("s_out")
        s_apart = sem("s_apart")
        s_ready = sem("s_ready")
        s_score = sem("s_score")
        s_sread = sem("s_sread")
        s_nm = sem("s_nm")
        s_exp = sem("s_exp")
        s_w = sem("s_w")
        s_t = sem("s_t")
        s_pt = sem("s_pt")
        s_pv = sem("s_pv")
        s_o = sem("s_o")
        sems = {n: sem(f"lane_{n}") for n in ("pe", "act", "dve", "pool", "sp")}
        block = ctx.enter_context(nc.Block())

        def v(name, k=0, n=1):
            return vec[:, VEC[name] + k:VEC[name] + k + n]

        def vdyn(name, k, n=1):
            return vec[:, bass.ds(VEC[name] + k, n)]

        def program(L):
            pe, act, dve, pool, sp = (L.name == n for n in ("pe", "act", "dve", "pool", "sp"))
            e = L.e
            done = L.done
            U = [0]
            BK = [0, 0, 0, 0]
            NX, NS, NB, NW, AT = [0], [0], [0], [0], [0]

            def need(ev, it=None):
                who, value, in_loop = counted["events"].get(ev, ("dve", 1, None))
                if in_loop is not None:
                    value = value + (L.i if it is None else it) * counted["per_iteration"][in_loop]
                e.wait_ge(sems[who], value)

            def loop(n, *lanes):
                return L.loop(n) if L.name in lanes else _skip()

            def place(u0, it, q):
                return (u0 + q) % 2, (u0 + q) // 2 + it

            def split(u0, it, q):
                p, k = place(u0, it, q)
                if act:
                    e.wait_ge(s_raw[p], 16 * (k + 1))
                    e.wait_ge(s_unit, 2 * k + p - 1)
                    e.activation(wh[p][:], raw[p][:], ACT.Copy).then_inc(s_hi, 1)
                if dve:
                    e.wait_ge(s_hi, 2 * k + p + 1)
                    e.tensor_tensor(wl[p][:], raw[p][:], wh[p][:].bitcast(F32), ALU.subtract)\
                     .then_inc(s_lo, 1)

            def mm3(out, p, blk, xhi, xlo, start, stop, M=P):
                e.matmul(out, wl[p][:, blk, 0:M], xhi, start=start, stop=False)
                e.matmul(out, wh[p][:, blk, 0:M], xlo, start=False, stop=False)
                return e.matmul(out, wh[p][:, blk, 0:M], xhi, start=False, stop=stop)

            def half(u0, it, q, bank, used, part):
                if pe:
                    p, k = place(u0, it, q)
                    if part == 0:
                        e.wait_ge(s_lo, 2 * k + p + 1)
                        e.wait_ge(s_bank[bank], used + 1)
                    for kt in range(KD // 2 * part, KD // 2 * (part + 1)):
                        mm = mm3(ps[bank][:], p, kt, xh[:, kt, :], xl[:, kt, :], kt == 0, kt == KD - 1)
                    if part:
                        mm.then_inc(s_unit, 1)

            def unit_pe(u0, it, q, parts, before=None):
                if not pe:
                    return
                p, k = place(u0, it, q)
                e.wait_ge(s_lo, 2 * k + p + 1)
                for bank, used, blks, tiles, (hi, lo) in parts:
                    e.wait_ge(s_bank[bank], used + 1)
                    for n, (blk, kt) in enumerate(zip(blks, tiles)):
                        if before is not None:
                            before(kt)
                        mm = mm3(ps[bank][:], p, blk, hi[:, kt, :], lo[:, kt, :], n == 0, n == len(blks) - 1)
                mm.then_inc(s_unit, 1)

            def unit_read(u0, it, q):
                e.wait_ge(s_unit, u0 + 2 * it + q + 1)

            FULL = (range(UB), range(KD))

            def apart():
                e.sem_inc(s_apart, 1)

            def ada_sum(src, dst, ev, prod=None):
                if dve:
                    done(e.tensor_scalar(dst, src[:, 0, :], sm[:, SC:SC + 1], None, ALU.mult), ev + "0")
                    for k in range(1, KD):
                        need(f"{ev}{k - 1}")
                        i = e.scalar_tensor_tensor(dst, src[:, k, :], sm[:, SC + k:SC + k + 1], dst, ALU.mult, ALU.add)
                        if k < KD - 1:
                            done(i, f"{ev}{k}")
                    return i
                by_c = sm[:, SC:SC + KD].unsqueeze(2).to_broadcast([P, KD, 256])
                prod = prod if prod is not None else src
                done(e.tensor_tensor(prod, src, by_c, ALU.mult), ev + "p")
                src = prod
                need(ev + "p")
                done(e.tensor_tensor(src[:, 0:4, :], src[:, 0:4, :], src[:, 4:8, :], ALU.add), ev + "4")
                need(ev + "4")
                done(e.tensor_tensor(src[:, 0:2, :], src[:, 0:2, :], src[:, 2:4, :], ALU.add), ev + "2")
                need(ev + "2")
                return e.tensor_tensor(dst, src[:, 0, :], src[:, 1, :], ALU.add)

            def ada_columns(src):
                for c in range(2):
                    mm = e.matmul(ps[6][:, c:c + 1], src[:, P * c:P * c + P], ones[:, 0:1], start=True, stop=True)
                return mm

            panel = bA[:].rearrange("p a b -> p (a b)").rearrange("p (k n) -> p k n", k=KD)

            def ada_load(a):
                e.dma_start(panel, io["ada"][a]).then_inc(s_ada, 16)

            def ada_begin(s, a, prod=None):
                e.wait_ge(s_ada, 16 * (a - (ADA_FIRST - 1)))
                e.wait_ge(s_col, a - (ADA_FIRST - 1))
                ada_sum(panel, acc[:, 0, :], s + "acc", prod).then_inc(s_acc, 1)

            def ada_next(a):
                if act:
                    e.wait_ge(s_acc, a - (ADA_FIRST - 1))
                    ada_load(a + 1)

            def ada_end(a):
                if pe:
                    e.wait_ge(s_acc, a - (ADA_FIRST - 1))
                    e.wait_ge(s_mod, a - (ADA_FIRST - 1))
                    ada_columns(acc[:, 0, :]).then_inc(s_col, 1)
                if dve:
                    e.wait_ge(s_col, a - (ADA_FIRST - 2))
                    if isinstance(a, int):
                        dst, bias = mod[:, 2 * a:2 * a + 2], v("ada_b", 2 * a, 2)
                    else:
                        dst, bias = mod[:, bass.ds(2 * a, 2)], vdyn("ada_b", 2 * a, 2)
                    e.tensor_tensor(dst, ps[6][:, 0:2], bias, ALU.add).then_inc(s_mod, 1)

            def ada_stands(a):
                e.wait_ge(s_mod, a - (ADA_FIRST - 2))

            def stats(s, src, n, width, sq, out, free):
                odd = lambda k: k % 2 == 1 and n > 2
                if act or dve:
                    for ev in free:
                        need(*ev)
                for k in range(n):
                    if act and not odd(k):
                        done(e.activation(sq(k), src(k), ACT.Square), f"{s}sq{k}")
                    if dve and odd(k):
                        done(e.tensor_tensor(sq(k), src(k), src(k), ALU.mult), f"{s}sq{k}")
                        need(f"{s}sq{k}")
                        need(f"{s}sq{k - 1}")
                        done(e.tensor_tensor(sq(k), sq(k), sq(k - 1), ALU.add), f"{s}sp{k}")
                if act:
                    done(e.activation(sm[:, 62:63], v("eps"), ACT.Sqrt), s + "tb")
                if pe:
                    terms = [k for k in range(n) if odd(k)] if n > 2 else list(range(n))
                    for k in terms:
                        need(f"{s}sp{k}" if n > 2 else f"{s}sq{k}")
                        mm = e.matmul(ps[7][:], ones, sq(k), start=(k == terms[0]), stop=(k == terms[-1]))
                    done(mm, s + "sum")
                if act:
                    need(s + "sum")
                    done(e.activation(out, ps[7][:], ACT.Sqrt, scale=1.0 / width, bias=v("eps")), s + "root")
                if dve:
                    need(s + "root")
                    done(e.reciprocal(out, out), s + "rstd")

            def put(s, k, src, hi, lo):
                if act:
                    need(f"{s}y{k}")
                    if L.in_loop:
                        apart()
                    done(e.activation(hi, src, ACT.Copy), f"{s}hi{k}")
                if pool:
                    need(f"{s}hi{k}")
                    done(e.tensor_tensor(lo, src, hi.bitcast(F32), ALU.subtract), f"{s}lo{k}")

            def put_all(s, n, make, src, shift, hi, lo):
                for k in range(n + 1):
                    bias = shift(k) if shift and k < n and k % 2 else None
                    if dve and k < n:
                        make(k)
                        if shift and not k % 2:
                            need(f"{s}t{k}")
                            done(e.tensor_scalar(src(k), src(k), shift(k), None, ALU.add), f"{s}y{k}")
                    if act and k < n:
                        need(f"{s}y{k}")
                        if bias is not None:
                            i = e.activation(hi[:, k, :], src(k), ACT.Identity, bias=bias)
                        else:
                            i = e.activation(hi[:, k, :], src(k), ACT.Copy)
                        done(i, f"{s}hi{k}")
                    if pool and k % 2 == 0 and k < n:
                        need(f"{s}hi{k}")
                        done(e.tensor_tensor(lo[:, k, :], src(k), hi[:, k, :].bitcast(F32), ALU.subtract), f"{s}lo{k}")
                    if dve and k > 0 and k % 2 == 0:
                        m = k - 1
                        need(f"{s}hi{m}")
                        if shift:
                            i = e.scalar_tensor_tensor(lo[:, m, :], src(m), shift(m), hi[:, m, :].bitcast(F32),
                                                       ALU.add, ALU.subtract)
                        else:
                            i = e.tensor_tensor(lo[:, m, :], src(m), hi[:, m, :].bitcast(F32), ALU.subtract)
                        done(i, f"{s}lo{m}")

            def stand(s, n):
                need(f"{s}lo{n - 1}")
                if n > 1:
                    need(f"{s}lo{n - 2}")

            def norm(s, src, n, width, gain, shift, hi, lo, free, tmp, rstd, fresh=True):
                if fresh:
                    stats(s, src, n, width, tmp, rstd, free)
                if dve:
                    if fresh:
                        need(s + "rstd")
                    for ev in free:
                        need(*ev)
                if act:
                    e.wait_ge(s_unit, U[0])

                def make(k):
                    done(e.scalar_tensor_tensor(tmp(k), src(k), gain(k), rstd, ALU.mult, ALU.mult),
                         f"{s}{'y' if shift is None or k % 2 else 't'}{k}")
                put_all(s, n, make, tmp, shift, hi, lo)

            def by_tile(s):
                return lambda kt: need(f"{s}lo{kt}")

            def hk(k):
                return h[:, k, :]

            def last(s, n):
                if pe:
                    stand(s, n)

            def mod_gain(s, n, col, g):
                if dve:
                    done(e.scalar_tensor_tensor(gs[:, n, :], mod[:, col:col + KD], 1.0, g, ALU.add, ALU.mult), s + "gs")
                    need(s + "gs")

            first = [bA[:]] + [b[:, 4 * q:4 * q + 4, :] for b in (bC, bD) for q in range(2)] + [bS[:]]
            first = [t.rearrange("p a b -> p (a b)") for t in first]
            if sp:
                e.dma_start(vec[:], io["vec"]).then_inc(s_par, 16)
                e.dma_start(cst[:], io["cst"]).then_inc(s_par, 16)
                e.dma_start(h[:], io["x"]).then_inc(s_x, 16)
                for a in range(ADA_FIRST):
                    if a == len(first):
                        for k in range(2):
                            e.dma_start(raw[k][:], io["w"][k]).then_inc(s_raw[k], 16)
                    if a >= len(first):
                        need(f"i{a - len(first)}acc{KD - 1}")
                    e.dma_start(first[a % len(first)], io["ada"][a].rearrange("p a b -> p (a b)")).then_inc(s_a0[a], 16)
            if pe:
                for s_ in (*s_bank, s_score, s_col, s_mod):
                    e.sem_inc(s_, 1)
                for s_ in (s_sread, s_exp, s_t, s_pt, s_pv, s_o):
                    e.sem_inc(s_, 2)
            if act:
                e.wait_ge(s_par, 32)
                done(e.activation(sm[:, SC:SC + 8], v("c", 0, 8), ACT.Tanh, scale=0.5), "i_th")
                done(e.activation(sm[:, SLAM:SLAM + KW], v("lam", 0, KW), ACT.Exp, scale=-1.0), "i_el")
                need("i_el")
                done(e.activation(sm[:, SLAM:SLAM + KW], sm[:, SLAM:SLAM + KW], ACT.Ln, bias=ones[:, 0:1]), "i_sp")
            if dve:
                e.wait_ge(s_par, 32)
                need("i_th")
                done(e.scalar_tensor_tensor(sm[:, SC:SC + 8], sm[:, SC:SC + 8], 1.0, v("c", 0, 8), ALU.add, ALU.mult), "i_c1")
                need("i_c1")
                done(e.tensor_scalar(sm[:, SC:SC + 8], sm[:, SC:SC + 8], 0.5, None, ALU.mult), "i_c")
                need("i_sp")
                done(e.tensor_scalar(sm[:, SLAM:SLAM + KW], sm[:, SLAM:SLAM + KW], -LRU_C / 2, None, ALU.mult), "i_nsp")
                done(e.tensor_scalar(sm[:, SBA:SBA + KW], v("ga_b", 0, KW), 0.5, None, ALU.mult), "i_ba")
                done(e.tensor_scalar(sm[:, SBX:SBX + KW], v("gx_b", 0, KW), 0.5, None, ALU.mult), "i_bx")
                need("i_bx")
            if pe or pool:
                e.wait_ge(s_par, 32)
            if pool:
                need("i_c")
            bTk = lambda k: bT[:, k, :]
            if act or dve:
                e.wait_ge(s_x, 16)
            stats("n0", hk, KD, D, bTk, bT[:, 9, :], [])
            in_slot = {}
            for a in range(ADA_FIRST):
                slot = 2 if a % 3 == 2 else a % 3
                if pool if slot == 2 else dve:
                    e.wait_ge(s_a0[a], 16)
                    if slot in in_slot:
                        need(f"i{in_slot[slot]}adamm")
                    done(ada_sum(first[a % len(first)].rearrange("p (k n) -> p k n", k=KD), acc[:, slot, :], f"i{a}acc"),
                         f"i{a}acc{KD - 1}")
                in_slot[slot] = a
                if pe:
                    need(f"i{a}acc{KD - 1}")
                    if a:
                        need(f"i{a - 1}mod")
                    done(ada_columns(acc[:, slot, :]), f"i{a}adamm")
                for m in (a - 1, a) if a == ADA_FIRST - 1 else (a - 1,):
                    if dve and m >= 0:
                        need(f"i{m}adamm")
                        done(e.tensor_tensor(mod[:, 2 * m:2 * m + 2], ps[6][:, 0:2], v("ada_b", 2 * m, 2), ALU.add), f"i{m}mod")
                if act and a == len(first):
                    need(f"i{a}acc{KD - 1}")
                    ada_load(ADA_FIRST)
            if dve:
                need(f"i{ADA_FIRST - 1}mod")
            mod_gain("n0", 0, 8, v("norm1_g", 0, 8))
            norm("n0", hk, KD, D, lambda k: gs[:, 0, k:k + 1], lambda k: mod[:, k:k + 1], xh, xl,
                 [("n0gs",), ("n0rstd",)], bTk, bT[:, 9, :], fresh=False)
            for q in range(2):
                if act:
                    e.wait_ge(s_raw[q], 16)
                    e.activation(wh[q][:], raw[q][:], ACT.Copy).then_inc(s_hi, 1)
                if dve:
                    e.wait_ge(s_hi, q + 1)
                    e.tensor_tensor(wl[q][:], raw[q][:], wh[q][:].bitcast(F32), ALU.subtract).then_inc(s_lo, 1)

            if sp:
                with L.loop(io["units"] // 2 - 1) as i:
                    for p in range(2):
                        e.wait_ge(s_lo, 2 * i + p + 1)
                        e.dma_start(raw[p][:], io["w"][2 * i + (2 + p)]).then_inc(s_raw[p], 16)

            u0, b0, b1 = U[0], BK[0], BK[1]
            if pool:
                need(f"i{ADA_FIRST - 2}adamm")
                stand("n0", KD)
            prod = bT[:, 0:4, :].rearrange("p a b -> p (a b)").rearrange("p (k n) -> p k n", k=KD)
            if pe:
                need(f"i{ADA_FIRST - 1}mod")
            with loop(KW, "pe", "act", "dve", "pool") as it:
                if pool:
                    ada_begin("A", ADA_FIRST + it, prod)
                unit_pe(u0, it, 0, [(0, b0 + it if pe else 0, *FULL, (xh, xl))], before=by_tile("n0"))
                unit_pe(u0, it, 1, [(1, b1 + it if pe else 0, *FULL, (xh, xl))])
                if act:
                    unit_read(u0, it, 0)
                if act or dve:
                    split(u0 + 2, it, 0)
                if act:
                    need("Aconv0", it - 1)
                    e.activation(bS[:, 0, :], ps[0][:], ACT.Copy).then_inc(s_bank[0], 1)
                    need("Aaccp")
                    ada_load(it + (ADA_FIRST + 1))
                if dve:
                    e.wait_ge(s_bank[0], b0 + it + 2)
                    done(e.tensor_scalar(bD[:, it, :], bS[:, 0, :], vdyn("conv_w", it + 3 * KW), vdyn("conv_b", it + 0),
                                         ALU.mult, ALU.add), "Aconv3")
                    for j in (2, 1, 0):
                        need(f"Aconv{j + 1}")
                        done(e.scalar_tensor_tensor(bD[:, it, 3 - j:T], bS[:, 0, 0:T - 3 + j], vdyn("conv_w", it + j * KW),
                                                    bD[:, it, 3 - j:T], ALU.mult, ALU.add), f"Aconv{j}")
                if act:
                    unit_read(u0, it, 1)
                if act or dve:
                    split(u0 + 2, it, 1)
                if act:
                    need("Agelu", it - 1)
                    e.activation(bS[:, 1, :], ps[1][:], ACT.Copy).then_inc(s_bank[1], 1)
                    e.wait_ge(s_bank[1], b1 + it + 2)
                    done(e.activation(bS[:, 2, :], bS[:, 1, :], ACT.Square), "Ax2")
                    need("Aconv0")
                    apart()
                    done(e.activation(bh[:, it, :], bD[:, it, :], ACT.Copy), "Ahi")
                if dve:
                    need("Ax2")
                    done(e.tensor_scalar(bS[:, 2, :], bS[:, 2, :], 0.044715, 1.0, ALU.mult, ALU.add), "Ai1")
                    need("Ai1")
                    done(e.scalar_tensor_tensor(bS[:, 2, :], bS[:, 2, :], math.sqrt(2 / math.pi), bS[:, 1, :],
                                                ALU.mult, ALU.mult), "Ai2")
                    need("Ahi")
                    done(e.tensor_tensor(bl[:, it, :], bD[:, it, :], bh[:, it, :].bitcast(F32), ALU.subtract), "Alo")
                if act:
                    need("Ai2")
                    done(e.activation(bS[:, 3, :], bS[:, 2, :], ACT.Tanh), "Ath")
                if dve:
                    need("Ath")
                    done(e.scalar_tensor_tensor(bC[:, it, :], bS[:, 3, :], 1.0, bS[:, 1, :], ALU.add, ALU.mult), "Agelu")
                if pe or dve:
                    ada_end(ADA_FIRST + it)
            U[0] += 2 * KW
            BK[0] += KW
            BK[1] += KW

            prod_b = bT[:, 7:11, :].rearrange("p a b -> p (a b)").rearrange("p (k n) -> p k n", k=KD)
            if pool:
                ada_begin("B", ADA_FIRST + KW, prod_b)
            if act or dve:
                need("Baccp")
            u0 = U[0]
            groups = [list(range(g, min(g + 4, KW))) for g in range(0, KW, 4)]
            if act or pe:
                need("Alo", KW - 1)
                need("Agelu", KW - 1)

            def recur(m):
                if dve:
                    need(f"G{m}s")
                    done(e.tensor_tensor(bD[:, m, :], bD[:, m, :], bA[:, m % 4, :], ALU.mult), f"G{m}u")
                    need(f"G{m}u")
                    done(e.tensor_tensor_scan(bT[:, m, :], bT[:, m, :], bD[:, m, :], 0.0, ALU.mult, ALU.add), f"G{m}r")
                    need(f"G{m}r")
                    done(e.scalar_tensor_tensor(bC[:, m, :], bC[:, m, :], 0.5, bT[:, m, :], ALU.mult, ALU.mult),
                         f"Yy{m}" if m < 4 else f"Zy{m - 4}")
            for j in range(KW):
                ks = lru_tiles(j)
                ba, bx = j % 2, 2 + j % 2
                unit_pe(u0, 0, j, [(bk, BK[bk], [3 * g + k - j + 1 for k in ks], ks, (bh, bl))
                                   for g, bk in enumerate((ba, bx))])
                if act:
                    unit_read(u0, 0, j)
                split(u0 + 2, 0, j)
                t1, t2, sq = bS[:, j % 2, :], bS[:, 2 + j % 2, :], bA[:, j % 4, :]
                a, x = bT[:, j, :], bD[:, j, :]
                if act and j == 7:
                    e.wait_ge(s_acc, KW + 1)
                nsp = sm[:, SLAM + j:SLAM + j + 1]
                if act:
                    if j >= 2:
                        need(f"G{j - 2}v")
                    e.activation(t1, ps[ba][:], ACT.Tanh, scale=0.5, bias=sm[:, SBA + j:SBA + j + 1]).then_inc(s_bank[ba], 1)
                    e.activation(t2, ps[bx][:], ACT.Tanh, scale=0.5, bias=sm[:, SBX + j:SBX + j + 1]).then_inc(s_bank[bx], 1)
                    e.wait_ge(s_bank[ba], BK[ba] + 2)
                    done(e.activation(a, t1, ACT.Exp, scale=nsp, bias=nsp), f"G{j}a")
                    need(f"G{j}a")
                    done(e.activation(t1, t1, ACT.Tanh, scale=nsp, bias=nsp), f"G{j}th")
                if j >= 4:
                    recur(j - 4)
                if dve:
                    need(f"G{j}th")
                    e.wait_ge(s_bank[bx], BK[bx] + 2)
                    if j >= 4:
                        need(f"G{j - 4}u")
                    done(e.tensor_tensor(sq, a, a, ALU.mult), f"G{j}aa")
                    need(f"G{j}aa")
                    done(e.scalar_tensor_tensor(sq, sq, 1.0, t1, ALU.add, ALU.mult), f"G{j}q")
                    done(e.scalar_tensor_tensor(x, t2, 1.0, x, ALU.add, ALU.mult), f"G{j}v")
                BK[ba] += 1
                BK[bx] += 1
                if j == 3:
                    ada_end(ADA_FIRST + KW)
                if j == 7:
                    for m in groups[0]:
                        put("Y", m, bC[:, m, :], bh[:, m, :], bl[:, m, :])
                for g in groups:
                    if g[-1] != j:
                        continue
                    if act:
                        for m in g:
                            need(f"G{m}q")
                            done(e.activation(bA[:, m % 4, :], bA[:, m % 4, :], ACT.Sqrt, scale=-0.25), f"G{m}s")
            for m in range(KW - 4, KW):
                recur(m)
            U[0] += KW
            if act:
                need(f"G{KW - 1}u")
                ada_load(ADA_FIRST + KW + 1)
                e.wait_ge(s_unit, U[0])
            put_all("Z", KW - 4, lambda k: None, lambda k: bC[:, 4 + k, :], None, bh[:, 4:KW, :], bl[:, 4:KW, :])

            u0 = U[0]
            used = [BK[0], BK[1]]
            if dve:
                ada_stands(ADA_FIRST + KW)
            for j in range(KW):
                if pe:
                    p, k = place(u0, 0, j)
                    e.wait_ge(s_lo, 2 * k + p + 1)
                    for blk in range(UB):
                        m, kt = divmod(UB * j + blk, KW)
                        bk = m % 2
                        if m == 0:
                            need(f"Ylo{kt}" if kt < 4 else f"Zlo{kt - 4}")
                        if kt == 0:
                            e.wait_ge(s_bank[bk], used[bk] + m // 2 + 1)
                        mm = mm3(ps[bk][:], p, blk, bh[:, kt, :], bl[:, kt, :], kt == 0, kt == KW - 1)
                        if kt == KW - 1 and blk < UB - 1:
                            done(mm, f"Op{m}")
                    mm.then_inc(s_unit, 1)
                if j < 8 and j % 2 == 0:
                    panel_at = ADA_FIRST + KW + 1 + j // 2
                    if dve:
                        ada_begin(f"O{j // 2}", panel_at)
                    ada_next(panel_at)
                split(u0 + 2, 0, j)
                for blk in range(UB):
                    m, kt = divmod(UB * j + blk, KW)
                    if kt == KW - 1 and dve:
                        if blk < UB - 1:
                            need(f"Op{m}")
                        else:
                            unit_read(u0, 0, j)
                        e.scalar_tensor_tensor(h[:, m, :], ps[m % 2][:], mod[:, 16 + m:17 + m], h[:, m, :],
                                               ALU.mult, ALU.add).then_inc(s_bank[m % 2], 1)
                if j < 8 and j % 2:
                    ada_end(panel_at)
            U[0] += KW
            BK[0] += KD // 2
            BK[1] += KD // 2

            def h_ready():
                if act or dve:
                    e.wait_ge(s_bank[0], BK[0] + 1)
                    e.wait_ge(s_bank[1], BK[1] + 1)

            def mlp(s, g2, ada0):
                u0, b = U[0], list(BK)
                with loop(N_FF, "pe", "act", "dve", "pool") as c:
                    it0 = UB * c if not sp else 0
                    for n in range(2 * KD):
                        up, it, q = n < KD, (it0 + n // 2), n % 2
                        if ada0 is not None and q == 0 and dve:
                            ada_begin(f"{s}{n}", ada0 + it)
                        if up:
                            unit_pe(u0, it, q, [(q, b[q] + it if pe else 0, *FULL, (xh, xl))],
                                    before=by_tile(s + "n") if n == 0 else None)
                        else:
                            unit_pe(u0, it, q, [(q, b[q] + it if pe else 0, *FULL, (bh, bl))],
                                    before=by_tile(s) if n == KD else None)
                        if act or (dve and not up):
                            unit_read(u0, it, q)
                        if act or dve:
                            split(u0 + 2, it, q)
                        if up:
                            if act:
                                need(f"{s}y{(n - 2) % KD}", c - (n < 2))
                                e.activation(bS[:, q, :], ps[q][:], ACT.Relu).then_inc(s_bank[q], 1)
                            if dve:
                                e.wait_ge(s_bank[q], b[q] + it + 2)
                                need(f"{s}lo{(n - 2) % KD}", c - (n < 2))
                                done(e.tensor_tensor(bS[:, 2 + q, :], bS[:, q, :], bS[:, q, :], ALU.mult), f"{s}y{n}")
                            put(s, n, bS[:, 2 + q, :], bh[:, n, :], bl[:, n, :])
                        elif dve:
                            m = n - KD
                            if n == KD and ada0 is not None:
                                ada_stands(ada0)
                            e.scalar_tensor_tensor(h[:, m, :], ps[q][:], mod[:, g2 + m:g2 + m + 1], h[:, m, :],
                                                   ALU.mult, ALU.add).then_inc(s_bank[q], 1)
                        if ada0 is not None and q == 0 and act:
                            ada_next(ada0 + it)
                        if ada0 is not None and q == 1 and (pe or dve):
                            ada_end(ada0 + it)
                U[0] += 2 * KD * N_FF
                for q in range(2):
                    BK[q] += KD * N_FF

            def norm_mod(s, n, src_cols, gain, extra=(), region=bTk, rstd=bT[:, 9, :], fresh=True):
                sh, sc = src_cols
                h_ready()
                mod_gain(s, n, sc, gain)
                norm(s, hk, KD, D, lambda k: gs[:, n, k:k + 1], lambda k: mod[:, sh + k:sh + k + 1], xh, xl,
                     list(extra), region, rstd, fresh)

            if dve:
                ada_stands(ADA_FIRST + KW + 4)
            norm_mod("M0n", 1, (24, 32), v("norm2_g", 0, 8), [(f"Zy{KW - 5}",)])
            mlp("M0", 40, ADA_FIRST + KW + 5)
            o_tok = bD[:, 8, :].rearrange("p (i f) -> p i f", i=NT)
            o_feat, scratch = bD[:, 9, :], bD[:, 10, :]

            def attend(steps, it, before=0, parts=1, fill={}):
                AT[0] += 1
                at = f"at{AT[0]}"
                nx, ns = sum(len(st["q"]) for st in steps), len(steps)
                x0 = NX[0] + nx * before + nx * parts * it
                s0 = NS[0] + ns * before + ns * parts * it
                w0 = NW[0] + ns * before + ns * parts * it
                xs = [i * (nx // ns) for i in range(ns)]

                def scores(n):
                    st = steps[n]
                    if "ready" in st:
                        st["ready"]()
                    for m in range(len(st["q"])):
                        x = xs[n] + m
                        e.wait_ge(s_sread, x0 + (x + 1))
                        e.matmul(ps[2 + x % 2][:, 0:st["nk"]], st["q"][m], st["k"][m], start=True, stop=True)\
                         .then_inc(s_score, 1)

                def maximum(n):
                    st = steps[n]
                    for m in range(len(st["q"])):
                        x = xs[n] + m
                        sc, nm = bD[:, x % 2, 0:st["nk"]], sm[:, SNM + x % 4:SNM + x % 4 + 1]
                        e.wait_ge(s_score, x0 + (x + 2))
                        e.wait_ge(s_exp, x0 + (x + 1))
                        e.scalar_tensor_tensor(sc, ps[2 + x % 2][:, 0:st["nk"]], st["scale"], st["bias"],
                                               ALU.mult, ALU.add).then_inc(s_sread, 1)
                        e.wait_ge(s_sread, x0 + (x + 3))
                        done(e.tensor_reduce(nm, sc, AX, ALU.max), f"{at}_{n}{m}mx")
                        need(f"{at}_{n}{m}mx")
                        if st.get("sink") is not None:
                            i = e.tensor_scalar(nm, nm, st["sink"], -1.0, ALU.max, ALU.mult)
                        else:
                            i = e.tensor_scalar(nm, nm, -1.0, None, ALU.mult)
                        i.then_inc(s_nm, 1)

                def exponentials(n):
                    st = steps[n]
                    e.wait_ge(s_t, s0 + (n + 1))
                    for m in range(len(st["q"])):
                        x = xs[n] + m
                        c = x % 4
                        e.wait_ge(s_nm, x0 + (x + 1))
                        nm = sm[:, SNM + c:SNM + c + 1]
                        if st.get("sink") is not None:
                            apart()
                            done(e.activation(sm[:, SES + c:SES + c + 1], st["sink"], ACT.Exp, bias=nm), f"{at}_{n}es")
                        e.activation(bD[:, 2 + c, 0:st["nk"]], bD[:, x % 2, 0:st["nk"]], ACT.Exp, bias=nm,
                                     accum_out=sm[:, SRS + c:SRS + c + 1]).then_inc(s_exp, 1)

                def combine(n):
                    st = steps[n]
                    x = xs[n]
                    c = x % 4
                    e.wait_ge(s_exp, x0 + (x + 4))
                    ri = sm[:, SRI + c:SRI + c + 2]
                    done(e.reciprocal(ri, sm[:, SRS + c:SRS + c + 2]), f"{at}_{n}ri")
                    need(f"{at}_{n}ri")
                    p0, p1 = bD[:, 2 + c, 0:st["nk"]], bD[:, 3 + c, 0:st["nk"]]
                    done(e.tensor_scalar(p0, p0, ri[:, 0:1], None, ALU.mult), f"{at}_{n}p0")
                    done(e.tensor_scalar(ri[:, 1:2], ri[:, 1:2], st["lam"], None, ALU.mult), f"{at}_{n}lm")
                    need(f"{at}_{n}lm")
                    e.scalar_tensor_tensor(p0, p1, ri[:, 1:2], p0, ALU.mult, ALU.add).then_inc(s_w, 1)

                def turn(n):
                    st = steps[n]
                    x = xs[n]
                    if st.get("lam") is not None:
                        e.wait_ge(s_w, w0 + (n + 1))
                    else:
                        e.wait_ge(s_exp, x0 + (x + 3))
                    e.wait_ge(s_pt, s0 + (n + 1))
                    for b in range(st["nk"] // P):
                        mm = e.transpose(ps[4 + n % 2][:, P * b:P * b + P],
                                         bD[:, 2 + x % 4, P * b:P * b + P], ident)
                    mm.then_inc(s_t, 1)

                def turned(n):
                    st = steps[n]
                    e.wait_ge(s_t, s0 + (n + 3))
                    e.wait_ge(s_pv, s0 + (n + 1))
                    e.activation(bD[:, 6 + n % 2, 0:st["nk"]], ps[4 + n % 2][:, 0:st["nk"]], ACT.Copy)\
                     .then_inc(s_pt, 1)

                def values(n):
                    st = steps[n]
                    e.wait_ge(s_pt, s0 + (n + 3))
                    e.wait_ge(s_o, s0 + (n + 1))
                    nb = st["nk"] // P
                    for b in range(nb):
                        mm = e.matmul(ps[6 + n % 2][:, 0:st["dv"]], bD[:, 6 + n % 2, P * b:P * b + P], st["v"][b],
                                      start=(b == 0), stop=(b == nb - 1))
                    mm.then_inc(s_pv, 1)

                def results(n):
                    st = steps[n]
                    x = xs[n]
                    c = x % 4
                    src = ps[6 + n % 2][:, 0:st["dv"]]
                    if st.get("lam") is not None:
                        e.wait_ge(s_pv, s0 + (n + 3))
                        e.tensor_copy(st["o"], src).then_inc(s_o, 1)
                        return
                    rs, ri = sm[:, SRS + c:SRS + c + 1], sm[:, SRI + c:SRI + c + 1]
                    e.wait_ge(s_exp, x0 + (x + 3))
                    if st.get("sink") is not None:
                        done(e.tensor_tensor(rs, rs, sm[:, SES + c:SES + c + 1], ALU.add), f"{at}_{n}sk")
                        need(f"{at}_{n}sk")
                    done(e.reciprocal(ri, rs), f"{at}_{n}ri")
                    need(f"{at}_{n}ri")
                    e.wait_ge(s_pv, s0 + (n + 3))
                    e.tensor_scalar(st["o"], src, ri, None, ALU.mult).then_inc(s_o, 1)

                ahead = 3 - len(steps[0]["q"])
                for n in range(ahead):
                    if pe:
                        scores(n)
                    if dve:
                        maximum(n)
                for n in range(ns):
                    if pe:
                        if n + ahead < ns:
                            scores(n + ahead)
                        if n in fill:
                            fill[n][0]()
                        turn(n)
                        if n:
                            values(n - 1)
                    if act:
                        exponentials(n)
                        if n:
                            turned(n - 1)
                        if n - 1 in fill:
                            fill[n - 1][1]()
                    if dve:
                        if n + ahead < ns:
                            maximum(n + ahead)
                        if steps[n].get("lam") is not None:
                            combine(n)
                        if n - 1 in fill:
                            fill[n - 1][1]()
                        if n:
                            results(n - 1)
                if pe:
                    values(ns - 1)
                if act:
                    turned(ns - 1)
                if dve:
                    results(ns - 1)
                if act or dve:
                    if ns - 1 in fill:
                        fill[ns - 1][1]()

            def attended(steps, times):
                NX[0] += sum(len(st["q"]) for st in steps) * times
                NS[0] += len(steps) * times
                if steps[0].get("lam") is not None:
                    NW[0] += len(steps) * times

            def copy_out(bank, used, dst):
                if act:
                    e.activation(dst, ps[bank][:], ACT.Copy).then_inc(s_bank[bank], 1)

            def copied(bank, used):
                e.wait_ge(s_bank[bank], used + 2)

            def head_norm(s, bank, used, x, tmp, gain, out, between=lambda: None):
                if act:
                    copied(bank, used)
                    apart()
                    done(e.activation(tmp, x, ACT.Square), s + "hsq")
                between()
                if pe:
                    need(s + "hsq")
                    done(e.matmul(ps[bank][:], ones64, tmp, start=True, stop=True), s + "hsum")
                if act:
                    need(s + "hsum")
                    e.activation(tmp, ps[bank][:], ACT.Sqrt, scale=1.0 / HD, bias=v("eps")).then_inc(s_bank[bank], 1)
                if dve:
                    copied(bank, used + 1)
                    done(e.reciprocal(tmp, tmp), s + "hrs")
                    need(s + "hrs")
                    done(e.scalar_tensor_tensor(out, x, gain, tmp, ALU.mult, ALU.mult), s + "hn")

            def turn_tile(s, bank, used, src, ready):
                if pe:
                    ready()
                    e.wait_ge(s_bank[bank], used + 1)
                    for i in range(NT):
                        mm = e.transpose(ps[bank][:, P * i:P * i + P], src(i), ident)
                    done(mm, s + "tt")

            def by_block(ap):
                return ap.rearrange("p (i f) -> p i f", i=NT)

            if dve:
                ada_stands(N_ADA - 1)
            norm_mod("KV", 2, (96, 104), v("kv_norm_g", 0, 8))
            u0, b = U[0], list(BK)
            with loop(KD // 2, "pe", "act", "dve") as it:
                for q in range(2):
                    unit_pe(u0, it, q, [(q, b[q] + 2 * it, *FULL, (xh, xl))], before=None if q else by_tile("KV"))
                for q in range(2):
                    kt = bC[:, 2 * it + q, :] if L.name in ("pe", "act", "dve") else None
                    if act:
                        unit_read(u0, it, q)
                        need(f"K{q}hn", it - 1)
                        apart()
                    copy_out(q, b[q] + 2 * it, kt)
                    head_norm(f"K{q}", q, b[q] + 2 * it, kt, bS[:, q, :], v("k_g"), kt,
                              lambda: split(u0 + 2, it, q))
            U[0] += KD
            for q in range(2):
                BK[q] += KD
            vtok = bT[:, 0:8, :].rearrange("p a b -> p (a b)").rearrange("p (i f) -> p i f", i=NT)
            u0, b = U[0], list(BK)
            with loop(KD // 2, "pe", "act", "dve") as it:
                for q in range(2):
                    unit_pe(u0, it, q, [(q, b[q] + 2 * it, *FULL, (xh, xl))])
                for q in range(2):
                    if act:
                        unit_read(u0, it, q)
                        need(f"V{q}tt", it - 1)
                        if q == 0:
                            need("K1hn", KD // 2 - 1)
                    copy_out(q, b[q] + 2 * it, bS[:, q, :])
                    if act or dve:
                        split(u0 + 2, it, q)
                    turn_tile(f"V{q}", q, b[q] + 2 * it + 1, lambda i: bS[:, q, P * i:P * i + P],
                              lambda: None)
                    if dve:
                        need(f"V{q}tt")
                        if q == 0:
                            stand("KV", KD)
                        e.tensor_copy(vtok[:, :, bass.ds(2 * P * it + P * q, P)], by_block(ps[q][:]))\
                         .then_inc(s_bank[q], 1)
            U[0] += KD
            for q in range(2):
                BK[q] += KD

            bDk = lambda k: bD[:, k, :]
            mod_gain("Q", 3, 56, v("norm1_g", 8, 8))
            norm("Q", hk, KD, D, lambda k: gs[:, 3, k:k + 1], lambda k: mod[:, 48 + k:49 + k], xh, xl, [], bDk,
                 bT[:, 9, :], fresh=False)
            u0, b = U[0], list(BK)
            if act:
                need("V1tt", KD // 2 - 1)
            if act or dve or pe:
                stand("Q", KD)
            if pe:
                e.wait_ge(s_bank[0], b[0] + 1)
                e.wait_ge(s_bank[1], b[1] + 1)
            qts, kts = [bC[:, 8 + u, :] for u in range(2)], [bT[:, 8 + 2 * u, :] for u in range(2)]

            def bias_load(j, u):
                e.dma_start(bS[:, 2 * u:2 * u + 2, :], io["attn_bias"][j]).then_inc(s_bias, 16)

            def prepare(s, it, q, scored):
                u, j = q % 2, 2 * it + q
                used = b[u] + 3 * it + 3 * (q // 2)
                qt, kt = qts[u], kts[u]

                def first_half():
                    half(u0, it, q, u, used, 0)

                def second_half():
                    half(u0, it, q, u, used, 1)

                def evict():
                    if act:
                        unit_read(u0, it, q)
                        scored()
                    copy_out(u, used, qt)
                    if act:
                        copied(u, used)
                        done(e.activation(scratch, qt, ACT.Square), s + "hsq")
                    split(u0 + 2, it, q)

                def head_sums():
                    if pe:
                        need(s + "hsq")
                        done(e.matmul(ps[u][:], ones64, scratch, start=True, stop=True), s + "hsum")

                def finish():
                    if act:
                        need(s + "hsum")
                        e.activation(scratch, ps[u][:], ACT.Sqrt, scale=1.0 / HD, bias=v("eps")).then_inc(s_bank[u], 1)
                    if dve:
                        copied(u, used + 1)
                        done(e.reciprocal(scratch, scratch), s + "hrs")
                        need(s + "hrs")
                        done(e.scalar_tensor_tensor(qt, qt, v("q_g"), scratch, ALU.mult, ALU.mult), s + "hn")
                        scored()
                        e.tensor_copy(kt, bC[:, j, :]).then_inc(s_ready, 1)
                return (first_half, lambda: None), (second_half, evict), (head_sums, finish)

            def chunk_pair(s, it, u, prev, fill, more):
                j = 2 * it + u
                used = b[u] + 3 * it
                if act and more:
                    e.wait_ge(s_sread, NX[0] + 16 * it + (8 * u + 2))
                    e.wait_ge(s_bias, 16 * j + 16)
                    bias_load(j + 1, 1 - u)
                if pe:
                    e.wait_ge(s_ready, j + 1)
                steps = []
                for g in range(2):
                    for i in range(NT):
                        nk, r = P * (i + 1), slice(HD * g, HD * g + HD)
                        at = P * j + HD * g
                        cols_ = slice(at, at + HD) if isinstance(j, int) else bass.ds(at, HD)
                        steps.append(dict(
                            q=[qts[u][r, P * i:P * i + P]], k=[kts[u][r, 0:nk]], nk=nk, scale=HD ** -0.5,
                            bias=bS[:, 2 * u + g, T - nk:T], dv=HD, o=o_tok[:, i, HD * g:HD * g + HD],
                            v=[vtok[:, m, cols_] for m in range(i + 1)]))
                if dve:
                    e.wait_ge(s_bias, 16 * j + 16)
                    prev("tt")
                attend(steps, it, u, 2, fill=fill)

                def ready():
                    e.wait_ge(s_o, NS[0] + 16 * it + (8 * u + 8 + 2))
                turn_tile(s, u, used + 2, lambda i: o_tok[:, i, :], ready)
                if act:
                    need(s + "tt")
                    prev("olo")
                    copy_out(u, used + 2, o_feat)
                    copied(u, used + 2)
                    if L.in_loop:
                        apart()
                    done(e.activation(bh[:, j, :], o_feat, ACT.Copy), s + "ohi")
                if pool:
                    need(s + "ohi")
                    done(e.tensor_tensor(bl[:, j, :], o_feat, bh[:, j, :].bitcast(F32), ALU.subtract), s + "olo")

            if act:
                bias_load(0, 0)
            for products, rest in prepare("Qp", 0, 0, lambda: None):
                products()
                rest()

            def pair_of(it, u, s, prev, last=False):
                def scored():
                    e.wait_ge(s_score, NX[0] + 16 * it + (8 * u + 1))
                fill = {} if last else dict(zip((1, 3, 5), prepare(f"{s}P{u}", it, u + 1, scored)))
                chunk_pair(f"{s}{u}", it, u, prev, fill, not last)
            with loop(KD // 2 - 1, "pe", "act", "dve", "pool") as it:
                if not sp:
                    pair_of(it, 0, "Q", lambda ev: need("Q1" + ev, it - 1))
                    pair_of(it, 1, "Q", lambda ev: need("Q0" + ev))
            if not sp:
                it = KD // 2 - 1
                pair_of(it, 0, "Ql", lambda ev: need("Q1" + ev, it - 1))
                pair_of(it, 1, "Ql", lambda ev: need("Ql0" + ev), last=True)
            U[0] += KD
            for q in range(2):
                BK[q] += 3 * KD // 2
            NX[0] += 64
            NS[0] += 64
            NB[0] += 8

            def residual(s, gcol):
                u0, b = U[0], list(BK)
                with loop(KD // 2, "pe", "act", "dve") as it:
                    for q in range(2):
                        unit_pe(u0, it, q, [(q, b[q] + it, *FULL, (bh, bl))])
                        if act:
                            unit_read(u0, it, q)
                        if dve:
                            unit_read(u0, it, q)
                        split(u0 + 2, it, q)
                        if dve:
                            e.scalar_tensor_tensor(h[:, 2 * it + q, :], ps[q][:], mod[:, bass.ds(2 * it + (gcol + q), 1)],
                                                   h[:, 2 * it + q, :], ALU.mult, ALU.add).then_inc(s_bank[q], 1)
                U[0] += KD
                for q in range(2):
                    BK[q] += KD // 2

            if pe:
                need("Ql1olo")
            residual("AO", 64)
            norm_mod("M1n", 4, (72, 80), v("norm2_g", 8, 8), [("Ql1olo",)])
            mlp("M1", 88, None)

            R = slice(ROPE0, MLA_QK)
            cos_t, sin_t, t0, t1 = bA[R, 0, :], bA[R, 1, :], bA[R, 2, :], bA[R, 3, :]
            if act:
                e.wait_ge(s_ada, 16 * (N_ADA - ADA_FIRST + 1))
                e.dma_start(t0.bitcast(I32), io["pos"]).then_inc(s_aux, 16)
            if dve:
                e.wait_ge(s_aux, 16)
                done(e.tensor_copy(sin_t, t0.bitcast(I32)), "R0")
                need("R0")
                invf = vec[R, VEC["inv_freq"]:VEC["inv_freq"] + 1]
                done(e.tensor_scalar(sin_t, sin_t, invf, None, ALU.mult), "R1")
                need("R1")
                done(e.tensor_scalar(t0.bitcast(I32), sin_t, 1 / (2 * math.pi), None, ALU.mult), "R2")
                need("R2")
                done(e.tensor_copy(t1, t0.bitcast(I32)), "R3")
                prev = "R3"
                for n, part in enumerate(TWO_PI):
                    need(prev)
                    done(e.scalar_tensor_tensor(sin_t, t1, -part, sin_t, ALU.mult, ALU.add), f"R4{n}")
                    prev = f"R4{n}"
                need(prev)
                done(e.tensor_scalar(cos_t, sin_t, math.pi / 2, None, ALU.add), "R5")
                need("R5")
                done(e.tensor_scalar(t0, cos_t, PI_IN, 2 * math.pi, ALU.is_gt, ALU.mult), "R6")
                need("R6")
                done(e.tensor_tensor(cos_t, cos_t, t0, ALU.subtract), "R7")
                need("R7")
                for n, t in enumerate((cos_t, sin_t)):
                    done(e.tensor_scalar(t, t, PI_IN, -PI_IN, ALU.min, ALU.max), f"R8{n}")
            if act:
                need("R81")
                for t in (cos_t, sin_t):
                    done(e.activation(t, t, ACT.Sin), "R9")
            if dve or act or pe:
                need("R9")

            def rotate(s, bank, used, x, out, tmp):
                if pe:
                    e.wait_ge(s_bank[bank], used + 1)
                    done(e.matmul(ps[bank][:], swap, x, start=True, stop=True), s + "rs")
                if dve:
                    need(s + "rs")
                    e.tensor_tensor(tmp[R, :], ps[bank][R, :], sin_t, ALU.mult).then_inc(s_bank[bank], 1)
                    done(e.tensor_tensor(out[R, :], x[R, :], cos_t, ALU.mult), s + "rc")
                    need(s + "rc")
                    done(e.tensor_tensor(out[R, :], out[R, :], tmp[R, :], ALU.add), s + "ro")
                    need(s + "ro")

            def gate_result(s, t, z, th):
                if dve:
                    need(s + "th")
                    done(e.scalar_tensor_tensor(th, th, 1.0, z, ALU.add, ALU.mult), s + "zz")
                    need(s + "zz")
                    done(e.scalar_tensor_tensor(o_feat, th, 0.5, o_feat, ALU.mult, ALU.mult), s + "y0")
                put(s, 0, o_feat, bh[:, t, :], bl[:, t, :])

            for l in range(2):
                lam_init = 0.8 - 0.6 * math.exp(-0.3 * l)
                n = f"L{l}"
                h_ready()
                norm(n + "n", hk, KD, D, lambda k: v("pre_g", 8 * l + k), None, xh, xl,
                     [(f"L{l - 1}end",)] if l else [("R9",)], bTk, bT[:, 9, :])
                if dve:
                    dl = v("da_l", 256 * l, 256).rearrange("p (a d) -> p a d", a=4)
                    for m in range(2):
                        done(e.tensor_tensor(scratch[:, HD * m:HD * m + HD], dl[:, 2 * m, :], dl[:, 2 * m + 1, :], ALU.mult), n + "l0")
                    need(n + "l0")
                    for m in range(2):
                        done(e.tensor_reduce(sm[:, SLN + m:SLN + m + 1], scratch[:, HD * m:HD * m + HD], AX, ALU.add), n + "l1")
                if act:
                    need(n + "l1")
                    done(e.activation(sm[:, SLN:SLN + 2], sm[:, SLN:SLN + 2], ACT.Exp), n + "l2")
                if dve:
                    need(n + "l2")
                    done(e.tensor_tensor(sm[:, SLN + 2:SLN + 3], sm[:, SLN + 1:SLN + 2], sm[:, SLN:SLN + 1], ALU.subtract), n + "l3")
                    need(n + "l3")
                    done(e.tensor_scalar(sm[:, SLN + 2:SLN + 3], sm[:, SLN + 2:SLN + 3], lam_init, None, ALU.subtract), n + "l4")
                    need(n + "l4")
                if act or dve or pe:
                    stand(n + "n", KD)

                early = [bT[:, 8, :], bT[:, 9, :], bT[:, 10, :], bC[:, 6, :]]

                def early_gate(s, u0, m, bank, used, wait=None):
                    def products(part=None):
                        for x in (0, 1) if part is None else (part,):
                            half(u0, 0, m, bank, used, x)

                    def rest():
                        if act:
                            unit_read(u0, 0, m)
                            if wait:
                                wait()
                            e.activation(early[m], ps[bank][:], ACT.Tanh, scale=0.5).then_inc(s_bank[bank], 1)
                        split(u0 + 2, 0, m)
                    return products, rest

                def branch_sum(s, first_branch, stand_event):
                    u0, b = U[0], list(BK)
                    adds = [None, None]
                    n, uses, wbs = 0, [0, 0], 0
                    for kind in ("gates4", "sum0", "sum2", "sum4", "gates6", "sum6"):
                        m0 = int(kind[-1])
                        if kind[:-1] == "gates":
                            for m in range(2):
                                unit_pe(u0, 0, n, [(m, b[m] + uses[m], *FULL, (xh, xl))])
                                if act:
                                    unit_read(u0, 0, n)
                                    if m0 == 6:
                                        e.wait_ge(s_bank[2 + m], b[2 + m] + wbs + 1)
                                    e.activation(bS[:, m, :], ps[m][:], ACT.Tanh, scale=0.5).then_inc(s_bank[m], 1)
                                split(u0 + 2, 0, n)
                                uses[m] += 1
                                n += 1
                            continue
                        if pe and m0 == 0:
                            need(stand_event)
                        if pe:
                            p, k = place(u0, 0, n)
                            e.wait_ge(s_lo, 2 * k + p + 1)
                            for m in range(2):
                                e.wait_ge(s_bank[2 + m], b[2 + m] + wbs + 1)
                                for kt in range(4):
                                    mm = mm3(ps[2 + m][:], p, 4 * m + kt, bh[:, kt, :], bl[:, kt, :], kt == 0, kt == 3)
                                if m == 0:
                                    done(mm, f"{s}half{wbs}")
                            mm.then_inc(s_unit, 1)
                        if act:
                            unit_read(u0, 0, n)
                            split(u0 + 2, 0, n)
                        for m in range(2):
                            if dve and m == 0:
                                need(f"{s}half{wbs}")
                            elif dve:
                                unit_read(u0, 0, n)
                            th = early[m0 + m] if m0 < 4 else bS[:, m, :]
                            y = bT[:, m0 + m, :]
                            if dve:
                                e.wait_ge(s_bank[m], b[m] + uses[m] + 1)
                                if not first_branch and adds[m]:
                                    need(adds[m])
                                e.scalar_tensor_tensor(y if first_branch else bS[:, 2 + m, :], th, 1.0,
                                                       ps[2 + m][:], ALU.add, ALU.mult).then_inc(s_bank[2 + m], 1)
                            if not first_branch:
                                adds[m] = f"{s}add{m0 + m}"
                                if pool:
                                    e.wait_ge(s_bank[2 + m], b[2 + m] + wbs + 2)
                                    done(e.tensor_tensor(y, y, bS[:, 2 + m, :], ALU.add), adds[m])
                        if dve:
                            split(u0 + 2, 0, n)
                        wbs += 1
                        n += 1
                    U[0] += 8
                    for q in range(4):
                        BK[q] += (2, 2, 4, 4)[q]

                def gate_up(s, th, z_in, z, ready):
                    if act:
                        ready("act")
                        done(e.activation(th, z_in, ACT.Tanh, scale=0.5), s + "th")
                    if dve:
                        need(s + "th")
                        ready("dve")
                        done(e.scalar_tensor_tensor(z, th, 1.0, z_in, ALU.add, ALU.mult), s + "zz")

                def gated(s, t, z):
                    if dve:
                        done(e.scalar_tensor_tensor(o_feat, z, 0.5, o_feat, ALU.mult, ALU.mult), s + "y0")
                    put(s, 0, o_feat, bh[:, t, :], bl[:, t, :])

                s0 = n + "D"
                qt, kt, vt, vk, zt, th, zn = (bC[:, k, :] for k in range(7))
                vk = by_block(vk)
                if act:
                    e.dma_start(bC[:, 7:11, :], io["da_bias"]).then_inc(s_bias, 16)
                NB[0] += 1
                u0, b = U[0], list(BK)
                for q, dst in enumerate((vt, zn, qt, kt)):
                    unit_pe(u0, 0, q, [(q % 2, b[q % 2] + q // 2, *FULL, (xh, xl))])
                    if act:
                        unit_read(u0, 0, q)
                    split(u0 + 2, 0, q)
                    copy_out(q % 2, b[q % 2] + q // 2, dst)
                U[0] += 4
                BK[0] += 2
                BK[1] += 2
                if dve:
                    e.wait_ge(s_bias, 16 * NB[0])
                u0, b = U[0], list(BK)

                def da_head(it, s, prev, units, u0, reg):
                    c0, c1 = b[0] + 4 * it, b[1] + 2 * it
                    turn_tile(s + "tt0", 0, c0, lambda i: vt[:, P * i:P * i + P], lambda: None)
                    if dve:
                        need(s + "tt0tt")
                        e.tensor_copy(vk, by_block(ps[0][:])).then_inc(s_bank[0], 1)

                    def ready(who):
                        if who == "act":
                            e.wait_ge(s_bank[1], c1 + 1)
                            prev("zz")
                        else:
                            prev("y0")
                    gate_up(s, th, zn, zt, ready)
                    steps = []
                    for i in range(NT):
                        nk = P * (i + 1)
                        steps.append(dict(q=[qt[HD * m:HD * m + HD, P * i:P * i + P] for m in range(2)],
                                          k=[kt[HD * m:HD * m + HD, 0:nk] for m in range(2)], nk=nk, scale=HD ** -0.5,
                                          bias=bC[:, 7 + it, T - nk:T], dv=P, o=o_tok[:, i, :], lam=sm[:, SLN + 2:SLN + 3],
                                          v=[vk[:, m, :] for m in range(i + 1)]))
                    fill = units(it, c0 + 1, c1)
                    if pe:
                        e.wait_ge(s_bank[1], c1 + 1)
                    if dve:
                        prev("tt1tt")
                    attend(steps, reg, fill={k: fill[k] for k in range(3)})
                    if pe:
                        fill[3][0]()
                    if act:
                        e.wait_ge(s_o, NS[0] + 4 * reg + (4 + 2))
                        for i in range(NT):
                            done(e.activation(bD[:, 0, P * i:P * i + P], o_tok[:, i, :], ACT.Square,
                                              accum_out=sm[:, SSQ + i:SSQ + i + 1]), s + "ssq")
                        need(s + "ssq")
                        done(e.activation(sm[:, SSQ:SSQ + NT], sm[:, SSQ:SSQ + NT], ACT.Sqrt, scale=1.0 / P, bias=v("eps")), s + "srt")
                        fill[3][1]()
                    if dve:
                        need(s + "srt")
                        done(e.reciprocal(sm[:, SSQ:SSQ + NT], sm[:, SSQ:SSQ + NT]), s + "srs")
                        need(s + "srs")
                        for i in range(NT):
                            done(e.tensor_scalar(o_tok[:, i, :], o_tok[:, i, :], sm[:, SSQ + i:SSQ + i + 1], None, ALU.mult), s + "sub")
                    turn_tile(s + "tt1", 0, c0 + 3, lambda i: o_tok[:, i, :], lambda: need(s + "sub"))
                    if dve:
                        need(s + "tt1tt")
                        prev("lo0")
                        e.tensor_scalar(o_feat, ps[0][:], v("subln", l), 1.0 - lam_init, ALU.mult, ALU.mult)\
                         .then_inc(s_bank[0], 1)
                        copied(0, c0 + 3)
                    gated(s, it, zt)
                    if dve:
                        fill[3][1]()

                def next_head(it, c0, c1):
                    s, out = s0, []
                    for q, (bank, used, dst) in enumerate([(0, c0, vt), (1, c1, zn), (0, c0 + 1, qt), (1, c1 + 1, kt)]):
                        def products(q=q, bank=bank, used=used):
                            for part in range(2):
                                half(u0, 2 * it, q, bank, used, part)

                        def rest(q=q, bank=bank, used=used, dst=dst):
                            if act:
                                unit_read(u0, 2 * it, q)
                                if q < 2:
                                    need(s + ("tt0tt", "zz")[q])
                                else:
                                    e.wait_ge(s_score, NX[0] + 8 * it + 9)
                            copy_out(bank, used, dst)
                            split(u0 + 2, 2 * it, q)
                        out.append((products, rest))
                    return out
                with loop(3, "pe", "act", "dve", "pool") as it:
                    if not sp:
                        da_head(it, s0, lambda ev: need(s0 + ev, it - 1), next_head, u0, it)
                U[0] += 12
                ug = U[0]
                if not sp:
                    da_head(3, s0 + "l", lambda ev: need(s0 + ev, 2), lambda it, c0, c1: [
                        early_gate(s0, ug, m, m % 2, (c0, c1)[m % 2] + m // 2,
                                   (lambda: need(s0 + "lzz")) if m == 3 else None) for m in range(4)], ug, 3)
                attended([dict(q=[0, 0], lam=1)] * NT, 4)
                U[0] += 4
                BK[0] += 16
                BK[1] += 8
                branch_sum(n + "E", True, s0 + "llo0")

                s = n + "B"
                u0, b = U[0], list(BK)
                for q in range(4):
                    unit_pe(u0, 0, q, [(q % 2, b[q % 2] + q // 2, *FULL, (xh, xl))])
                    if act:
                        unit_read(u0, 0, q)
                        if q == 0:
                            e.wait_ge(s_bank[2], b[2] + 1)
                            e.wait_ge(s_bank[3], b[3] + 1)
                    split(u0 + 2, 0, q)
                    copy_out(q % 2, b[q % 2] + q // 2, bS[:, q, :])
                U[0] += 4
                for q in range(2):
                    BK[q] += 2
                if act or dve or pe:
                    copied(0, BK[0] - 1)
                    copied(1, BK[1] - 1)
                norm(s + "q", lambda k: bS[:, k, :], 2, 2 * P, lambda k: v("mq_g", 2 * l + k), None,
                     bh[:, 8:10, :], bl[:, 8:10, :], [], lambda k: bC[:, k, :], bC[:, 2, :])
                norm(s + "k", lambda k: bS[:, 2, :], 1, P, lambda k: v("mkv_g", l), None,
                     bh[:, 10:11, :], bl[:, 10:11, :], [(s + "qlo0",), (s + "qlo1",)], lambda k: bC[:, 3, :], bC[:, 4, :])
                ks = [bA[:, 2, :], bA[:, 3, :]]
                rotate(s + "r", 0, BK[0], bS[:, 3, :], ks[0], scratch)
                if dve:
                    need(s + "rro")
                    done(e.tensor_copy(ks[1][R, :], ks[0][R, :]), s + "rk")
                BK[0] += 1
                if act:
                    need(s + "rk")
                    e.dma_start(bC[:, 10, :], io["mask"]).then_inc(s_bias, 16)
                last(s + "q", 2)
                last(s + "k", 1)
                NB[0] += 1
                u0, b = U[0], list(BK)
                qn, kv, qt = ([bC[:, k + g, :] for g in range(2)] for k in (0, 2, 4))
                zn, th, zt, vk, mask = (bC[:, k, :] for k in range(6, 11))
                vk = by_block(vk)
                qk_hl, kv_hl = (bh[:, 8:10, :], bl[:, 8:10, :]), (bh[:, 10:11, :], bl[:, 10:11, :])

                def low_rank(s, u0, it, g, c0, c1, ready):
                    def products():
                        if pe:
                            if g == 0:
                                p, k = place(u0, it, 0)
                                e.wait_ge(s_lo, 2 * k + p + 1)
                            else:
                                p = place(u0, it, 0)[0]
                            e.wait_ge(s_bank[0], c0 + (g + 1))
                            for m in range(2):
                                mm = mm3(ps[0][:], p, 2 * g + m, qk_hl[0][:, m, :], qk_hl[1][:, m, :], m == 0, m == 1)
                            done(mm, f"{s}q{g}")
                            e.wait_ge(s_bank[1], c1 + (g + 1))
                            mm = mm3(ps[1][:], p, 4 + g, kv_hl[0][:, 0, :], kv_hl[1][:, 0, :], True, True)
                            if g:
                                mm.then_inc(s_unit, 1)
                            else:
                                done(mm, f"{s}k{g}")

                    def rest():
                        if act:
                            need(f"{s}q{g}")
                            ready(g)
                            copy_out(0, c0 + g, qn[g])
                            if g:
                                unit_read(u0, it, 0)
                            else:
                                need(f"{s}k{g}")
                            copy_out(1, c1 + g, kv[g])
                        if g and (act or dve):
                            split(u0 + 2, it, 0)
                    return products, rest

                for g in range(2):
                    products, rest = low_rank(s + "p", u0, 0, g, b[0], b[1], lambda g: (stand(s + "q", 2), stand(s + "k", 1)))
                    products()
                    rest()
                unit_pe(u0, 0, 1, [(0, b[0] + 2, *FULL, (xh, xl))])
                if act:
                    unit_read(u0, 0, 1)
                split(u0 + 2, 0, 1)
                copy_out(0, b[0] + 2, zn)
                U[0] += 2
                BK[0] += 3
                BK[1] += 2
                if dve:
                    e.wait_ge(s_bias, 16 * NB[0])
                u0, b = U[0], list(BK)
                s0 = s

                def mla_pair(it, s, prev, units, reg):
                    c0, c1 = b[0] + 5 * it, b[1] + 5 * it
                    if dve or pe:
                        e.wait_ge(s_bank[0], c0 + 1)
                        e.wait_ge(s_bank[1], c1 + 1)
                    if dve:
                        e.wait_ge(s_score, NX[0] + 8 * reg + 1)
                    def operands(g):
                        if dve:
                            done(e.tensor_copy(qt[g][0:HD, :], qn[g][0:HD, :]), f"{s}qc{g}")
                            done(e.tensor_copy(ks[g][0:HD, :], kv[g][0:HD, :]), f"{s}kc{g}")
                        rotate(f"{s}{g}", 0, c0 + g, qn[g], qt[g], scratch)
                        turn_tile(f"{s}t{g}", 1, c1 + g, lambda i: kv[g][:, P * i:P * i + P], lambda: None)
                        if dve:
                            need(f"{s}t{g}tt")
                            e.tensor_copy(vk[:, :, HD * g:HD * g + HD], by_block(ps[1][:])[:, :, HD:P])\
                             .then_inc(s_bank[1], 1)
                    operands(0)

                    def ready(who):
                        if who == "act":
                            e.wait_ge(s_bank[0], c0 + 1)
                            prev("zz")
                        else:
                            prev("y0")
                    gate_up(s, th, zn, zt, ready)
                    steps = []
                    for g in range(2):
                        for i in range(NT):
                            nk = P * (i + 1)
                            steps.append(dict(q=[qt[g][0:MLA_QK, P * i:P * i + P]], k=[ks[g][0:MLA_QK, 0:nk]], nk=nk,
                                              scale=MLA_QK ** -0.5, bias=mask[:, T - nk:T], dv=HD,
                                              o=o_tok[:, i, HD * g:HD * g + HD],
                                              v=[vk[:, m, HD * g:HD * g + HD] for m in range(i + 1)]))

                    def ready_1():
                        need(s + "1ro")
                        copied(1, c1 + 1)
                    steps[NT]["ready"] = ready_1
                    if pe:
                        need(s + "0ro")
                        copied(1, c1)
                    if dve:
                        prev("ot")

                    def stand_1():
                        if pe:
                            operands(1)
                    attend(steps, reg, fill={0: (stand_1, lambda: dve and operands(1)),
                                             **units(it, c0 + 2, c1 + 2)})
                    if pe:
                        e.wait_ge(s_o, NS[0] + 8 * reg + (8 + 2))
                        e.wait_ge(s_bank[1], c1 + 5)
                        for i in range(NT):
                            mm = e.transpose(ps[1][:, P * i:P * i + P], o_tok[:, i, :], ident)
                        done(mm, s + "ot")
                    if dve:
                        need(s + "ot")
                        prev("lo0")
                        e.tensor_copy(o_feat, ps[1][:]).then_inc(s_bank[1], 1)
                        copied(1, c1 + 4)
                    gated(s, it, zt)

                def next_pair(it, c0, c1):
                    s = s0

                    def ready(g):
                        need(f"{s}{g}rc")
                        need(f"{s}t{g}tt")
                    def products(part):
                        return lambda: half(u0, it, 1, 0, c0 + 2, part)

                    def rest():
                        if act:
                            unit_read(u0, it, 1)
                            need(s + "zz")
                        copy_out(0, c0 + 2, zn)
                        split(u0 + 2, it, 1)
                    return {1: low_rank(s, u0, it, 0, c0, c1, ready), 3: low_rank(s, u0, it, 1, c0, c1, ready),
                            4: (products(0), lambda: None), 6: (products(1), rest)}

                def early_gates(ug, c0, c1, last, first_step=0):
                    fill = {}
                    for m in range(4):
                        products, rest = early_gate(s0, ug, m, m % 2, (c0, c1)[m % 2] + m // 2, last if m == 3 else None)
                        if m == 3 and first_step:
                            fill[7] = products, rest
                            break
                        fill[2 * m + first_step] = (lambda products=products: products(0)), lambda: None
                        fill[2 * m + 1 + first_step] = (lambda products=products: products(1)), rest
                    return fill
                with loop(3, "pe", "act", "dve", "pool") as it:
                    if not sp:
                        mla_pair(it, s0, lambda ev: need(s0 + ev, it - 1), next_pair, it)
                U[0] += 6
                ug = U[0]
                if not sp:
                    mla_pair(3, s0 + "l", lambda ev: need(s0 + ev, 2),
                             lambda it, c0, c1: early_gates(ug, c0, c1, lambda: need(s0 + "lzz"), 1), 3)
                attended([dict(q=[0])] * 8, 4)
                U[0] += 4
                BK[0] += 19
                BK[1] += 20
                branch_sum(n + "F", False, s0 + "llo0")

                s0 = n + "S"
                u0, b = U[0], list(BK)
                kt, qt, vt, vk, zt, th, zn = (bC[:, k, :] for k in range(7))
                vk = by_block(vk)
                bi = bC[:, 7:11, :].rearrange("p a b -> p (a b)").rearrange("p (h k) -> p h k", h=8)
                if act:
                    need(n + "Bly0")
                    e.wait_ge(s_bank[2], b[2] + 1)
                    e.wait_ge(s_bank[3], b[3] + 1)
                    e.dma_start(bC[:, 7:11, :], io["sw_bias"]).then_inc(s_bias, 16)
                NB[0] += 1
                for q, dst in enumerate((kt, vt, qt, zn)):
                    unit_pe(u0, 0, q, [(q % 2, b[q % 2] + q // 2, *FULL, (xh, xl))])
                    if act:
                        unit_read(u0, 0, q)
                    split(u0 + 2, 0, q)
                    copy_out(q % 2, b[q % 2] + q // 2, dst)
                U[0] += 4
                BK[0] += 2
                BK[1] += 2
                if pe:
                    e.wait_ge(s_bank[0], BK[0] + 1)
                turn_tile(s0 + "v", 1, BK[1], lambda i: vt[:, P * i:P * i + P], lambda: None)
                if dve:
                    need(s0 + "vtt")
                    e.tensor_copy(vk, by_block(ps[1][:])).then_inc(s_bank[1], 1)
                BK[1] += 1
                if dve:
                    e.wait_ge(s_bias, 16 * NB[0])
                u0, b = U[0], list(BK)

                def sw_pair(it, s, prev, units, reg):
                    c0, c1 = b[0] + it, b[1] + 2 * it

                    def ready(who):
                        if who == "act":
                            e.wait_ge(s_bank[1], c1 + 1)
                            prev("zz")
                        else:
                            prev("y0")
                    gate_up(s, th, zn, zt, ready)
                    steps = []
                    for g in range(2):
                        r = slice(HD * g, HD * g + HD)
                        for i in range(NT):
                            k0 = P * max(i - 1, 0)
                            nk = P * (i + 1) - k0
                            at = 8 * l + 4 * g + it
                            steps.append(dict(q=[qt[r, P * i:P * i + P]], k=[kt[r, k0:k0 + nk]], nk=nk, scale=HD ** -0.5,
                                              bias=bi[:, 4 * g + it, 2 * P - nk:2 * P], dv=HD, o=o_tok[:, i, r],
                                              sink=v("sinks", at) if isinstance(it, int) else vdyn("sinks", at),
                                              v=[vk[:, m, r] for m in range(k0 // P, i + 1)]))
                    if pe:
                        e.wait_ge(s_bank[0], c0 + 1)
                        e.wait_ge(s_bank[1], c1 + 1)
                    if dve:
                        prev("ot")
                    fill, tail = units(it, c0, c1)
                    attend(steps, reg, fill=fill)
                    tail()
                    if pe:
                        e.wait_ge(s_o, NS[0] + 8 * reg + (8 + 2))
                    used = c1 + (1 if not isinstance(it, int) else 2)
                    if pe:
                        e.wait_ge(s_bank[1], used + 1)
                        for i in range(NT):
                            mm = e.transpose(ps[1][:, P * i:P * i + P], o_tok[:, i, :], ident)
                        done(mm, s + "ot")
                    if dve:
                        need(s + "ot")
                        prev("lo0")
                        e.tensor_copy(o_feat, ps[1][:]).then_inc(s_bank[1], 1)
                        copied(1, used)
                    gated(s, it, zt)

                def next_window(it, c0, c1):
                    def products(q, bank, used, part):
                        return lambda: half(u0, it, q, bank, used, part)

                    def rest(q, bank, used, dst):
                        def evaluate():
                            if act:
                                unit_read(u0, it, q)
                                if q == 0:
                                    need(s0 + "zz")
                                else:
                                    e.wait_ge(s_score, NX[0] + 8 * it + 9)
                            copy_out(bank, used, dst)
                            split(u0 + 2, it, q)
                        return evaluate
                    nothing = lambda: None
                    return {1: (products(0, 1, c1, 0), nothing), 3: (products(0, 1, c1, 1), rest(0, 1, c1, zn)),
                            6: (products(1, 0, c0, 0), nothing), 7: (products(1, 0, c0, 1), nothing)}, rest(1, 0, c0, qt)
                with loop(3, "pe", "act", "dve", "pool") as it:
                    if not sp:
                        sw_pair(it, s0, lambda ev: need(s0 + ev, it - 1), next_window, it)
                U[0] += 6
                ug = U[0]
                if not sp:
                    sw_pair(3, s0 + "l", lambda ev: need(s0 + ev, 2),
                            lambda it, c0, c1: (early_gates(ug, c0, c1, lambda: need(s0 + "lzz")), lambda: None), 3)
                attended([dict(q=[0])] * 8, 4)
                U[0] += 4
                BK[0] += 5
                BK[1] += 9
                branch_sum(n + "H", False, s0 + "llo0")

                s = n + "O"
                if act:
                    e.wait_ge(s_unit, U[0])
                    e.dma_start(bD[:, 0:2, :], io["ple"][l]).then_inc(s_aux, 16)
                if dve:
                    need(f"{n}Hadd7")

                def halve(k):
                    done(e.tensor_scalar(bT[:, k, :], bT[:, k, :], 0.5, None, ALU.mult), f"{s}y{k}")
                put_all(s, KD, halve, bTk, None, bh, bl)
                u0, b = U[0], list(BK)
                if act:
                    need(n + "Sly0")
                with loop(KD // 2, "pe", "act", "dve") as it:
                    for q in range(2):
                        unit_pe(u0, it, q, [(q, b[q] + it, *FULL, (bh, bl))], before=None if q else by_tile(s))
                        if act:
                            unit_read(u0, it, q)
                        if act or dve:
                            split(u0 + 2, it, q)
                        if act:
                            e.activation(bC[:, 2 * it + q, :], ps[q][:], ACT.Copy).then_inc(s_bank[q], 1)
                U[0] += KD
                for q in range(2):
                    BK[q] += KD // 2
                if act or dve:
                    e.wait_ge(s_bank[0], BK[0] + 1)
                    e.wait_ge(s_bank[1], BK[1] + 1)
                if dve:
                    e.wait_ge(s_aux, 32 + 16 * l)

                def copy(k):
                    done(e.tensor_copy(bC[:, 9 + k, :], bD[:, k, :]), f"{n}py{k}")
                put_all(n + "p", 2, copy, lambda k: bC[:, 9 + k, :], None, bh[:, 8:10, :], bl[:, 8:10, :])
                stats(s + "z", lambda k: bC[:, k, :], KD, D, lambda k: bD[:, 2 + k, :], bT[:, 9, :], [])
                if dve:
                    need(s + "zrstd")

                def add(k):
                    done(e.scalar_tensor_tensor(bC[:, k, :], bC[:, k, :], v("post_g", 8 * l + k), bT[:, 9, :],
                                                ALU.mult, ALU.mult), f"{s}n{k}")
                    need(f"{s}n{k}")
                    done(e.tensor_tensor(h[:, k, :], h[:, k, :], bC[:, k, :], ALU.add), f"{n}xy{k}")
                put_all(n + "x", KD, add, hk, None, xh, xl)

                u0, b = U[0], list(BK)
                last(n + "p", 2)
                if act:
                    stand(s, KD)
                for q in range(2):
                    if pe:
                        p, k = place(u0, 0, q)
                        e.wait_ge(s_lo, 2 * k + p + 1)
                        for m in range(4):
                            e.wait_ge(s_bank[m], b[m] + q + 1)
                            for kt in range(2):
                                mm = mm3(ps[m][:], p, 2 * m + kt, bh[:, 8 + kt, :], bl[:, 8 + kt, :], kt == 0, kt == 1)
                            if m < 3:
                                done(mm, f"{n}pp{q}{m}")
                        mm.then_inc(s_unit, 1)
                    if act:
                        for m in range(4):
                            if m < 3:
                                need(f"{n}pp{q}{m}")
                            else:
                                unit_read(u0, 0, q)
                            e.activation(bT[:, 4 * q + m, :], ps[m][:], ACT.Copy).then_inc(s_bank[m], 1)
                    split(u0 + 2, 0, q)
                U[0] += 2
                for m in range(4):
                    BK[m] += 2
                if dve:
                    for m in range(4):
                        e.wait_ge(s_bank[m], BK[m] + 1)
                if dve or pe:
                    stand(n + "x", KD)
                u0, b = U[0], list(BK)
                s = n + "P"
                with loop(KD // 2, "pe", "act", "dve") as it:
                    for q in range(2):
                        unit_pe(u0, it, q, [(q, b[q] + it, *FULL, (xh, xl))])
                        if act:
                            unit_read(u0, it, q)
                        if act or dve:
                            split(u0 + 2, it, q)
                        if act:
                            need(f"{s}m{q}", it - 1)
                            e.activation(bS[:, q, :], ps[q][:], ACT.Tanh, scale=0.5).then_inc(s_bank[q], 1)
                        if dve:
                            copied(q, b[q] + it)
                            done(e.scalar_tensor_tensor(bS[:, 2 + q, :], bS[:, q, :], 1.0, bT[:, 2 * it + q, :], ALU.add, ALU.mult), f"{s}m{q}")
                            need(f"{s}m{q}")
                            done(e.scalar_tensor_tensor(h[:, 2 * it + q, :], bS[:, 2 + q, :], 0.5, h[:, 2 * it + q, :], ALU.mult, ALU.add), f"{s}h{q}")
                U[0] += KD
                for q in range(2):
                    BK[q] += KD // 2
                if dve or act:
                    need(f"{s}h1", KD // 2 - 1)
                if dve:
                    done(e.tensor_copy(sm[:, 63:64], sm[:, 0:1]), f"L{l}end")
            if sp:
                need("L1end")
                e.dma_start(io["out"], h[:]).then_inc(s_out, 16)
                e.wait_ge(s_out, 16)
                for p in range(2):
                    e.wait_ge(s_raw[p], 16 * (io["units"] // 2))
            assert U[0] + 2 == io["units"], U[0]

        for eng, name in ((block.sync, "sp"), (block.tensor, "pe"), (block.scalar, "act"),
                          (block.vector, "dve"), (block.gpsimd, "pool")):
            @eng
            def _(e, name=name):
                program(Lane(name, e, sems[name], plan))


@contextmanager
def _skip():
    yield 0


def _stream(a):
    units, blocks = [], []

    def block(w=None, r=0, cols=None):
        b = np.zeros((P, P), np.float32)
        if w is not None:
            part = w[r:r + P, cols]
            b[:part.shape[0], :part.shape[1]] = part
        blocks.append(b)
        if len(blocks) == UB:
            units.append(np.stack(blocks, 1))
            blocks.clear()

    def cols(n, width=P):
        return slice(n, n + width)

    def column(w, c, k0=0, n=KD):
        for k in range(n):
            block(w, P * (k0 + k), c)

    w_in = a["lru_w_in"][0]
    for j in range(KW):
        column(w_in, cols(W + P * j))
        column(w_in, cols(P * j))
    gates = []
    for name in ("lru_gate_a_w", "lru_gate_x_w"):
        full = np.zeros((W, W), np.float32)
        for n, blk in enumerate(a[name][0]):
            full[LRU_BLK * n:LRU_BLK * (n + 1), LRU_BLK * n:LRU_BLK * (n + 1)] = blk
        gates.append(full)
    for j in range(KW):
        for full in gates:
            for k in (j - 1, j, j + 1):
                block(full if 0 <= k < KW else None, P * k, cols(P * j))
        block()
        block()
    for n in range(KD):
        column(a["lru_w_out"][0], cols(P * n), 0, KW)

    def mlp(l):
        for c in range(N_FF):
            for n in range(KD):
                column(a["mlp_w1"][l], cols(D * c + P * n))
            for n in range(KD):
                column(a["mlp_w2"][l], cols(P * n), KD * c)

    mlp(0)
    for n in range(2 * KD):
        column(a["kv_w"], cols(P * n))
    for w in (a["attn_w_q"][0], a["attn_w_o"][0]):
        for n in range(KD):
            column(w, cols(P * n))
    mlp(1)
    heads = [np.r_[HD * t:HD * (t + 1), HD * (t + 4):HD * (t + 5)] for t in range(4)]
    for l in range(2):
        w = a["w_in_2"][l]
        o = IN_OFF

        def branch(n, wb):
            for kind in ("gates0", "gates2", "gates4", "sum0", "sum2", "sum4", "gates6", "sum6"):
                m = int(kind[-1])
                for g in range(m, m + 2):
                    if kind[:-1] == "gates":
                        column(w, cols(o["g"] + D * n + P * g))
                    else:
                        column(wb, cols(P * g), 0, 4)

        for t in range(4):
            for name in ("av", "az", "aq", "ak"):
                column(w, cols(o[name] + P * t))
        branch(0, a["w_br_a_2"][l])
        for c in (cols(o["bq"]), cols(o["bq"] + P), cols(o["bkv"]), cols(o["bkr"] - ROPE0, MLA_QK)):
            column(w, c)
        for t in range(4):
            for g in range(2):
                for k in range(2):
                    block(a["mla_w_qb_2"][l], P * k, cols(MLA_QK * (2 * t + g), MLA_QK))
            for g in range(2):
                block(a["mla_w_kvb_2"][l], 0, cols(P * (2 * t + g)))
            block()
            block()
            column(w, cols(o["bz"] + P * t))
        branch(1, a["w_br_b_2"][l])
        column(w, cols(o["ck"]))
        column(w, cols(o["cv"]))
        for t in range(4):
            for name in ("cq", "cz") if t == 0 else ("cz", "cq"):
                column(w, o[name] + heads[t])
        branch(2, a["w_br_c_2"][l][np.concatenate(heads)])
        for n in range(KD):
            column(a["w_out_2"][l], cols(P * n))
        for n in range(KD):
            column(a["w_ple_proj_2"][l], cols(P * n), 0, 2)
        for n in range(KD):
            column(a["w_ple_gate_2"][l], cols(P * n))
    assert not blocks
    units += [np.zeros((P, UB, P), np.float32)] * 2
    return np.stack(units)


def _features(x):
    return np.ascontiguousarray(np.asarray(x).reshape(-1, P).T)


def _vectors(a):
    def rows(x):
        return np.broadcast_to(np.asarray(x).reshape(1, -1), (P, np.asarray(x).size))

    freq = np.zeros((P, 1), np.float32)
    half = (MLA_QK - ROPE0) // 2
    f = (np.float32(10000.0) ** (-np.arange(half, dtype=np.float32) / half)).astype(np.float32)
    freq[ROPE0:MLA_QK, 0] = np.concatenate([f, f])
    two = lambda x: np.concatenate([x, x])
    parts = dict(
        c=_features(a["c"]), ada_b=np.concatenate([_features(a["ada_b"]), _features(a["kv_ada_b"])], 1),
        norm1_g=_features(a["norm1_g"]), norm2_g=_features(a["norm2_g"]), kv_norm_g=_features(a["kv_norm_g"]),
        conv_w=_features(a["lru_conv_w"]), conv_b=_features(a["lru_conv_b"]), ga_b=_features(a["lru_gate_a_b"]),
        gx_b=_features(a["lru_gate_x_b"]), lam=_features(a["lru_lambda"]), k_g=_features(two(a["k_norm_g"])),
        q_g=_features(two(a["q_norm_g"][0])), pre_g=_features(a["norm_pre_2"]), post_g=_features(a["norm_post_2"]),
        mq_g=_features(a["mla_q_norm_2"]), mkv_g=_features(a["mla_kv_norm_2"]), subln=_features(a["da_subln_2"]),
        sinks=rows(a["sw_sinks_2"]), da_l=rows(a["da_lambda_2"]), inv_freq=freq,
        eps=np.full((P, 1), EPS, np.float32))
    return np.ascontiguousarray(np.concatenate([parts[k] for k in VEC], 1))


def _bucket(rel):
    n = np.maximum(rel, 0)
    nf = np.maximum(n, 1).astype(np.float32)
    large = 16 + (np.log(nf / np.float32(16)) / np.float32(math.log(128 / 16)) * np.float32(16)).astype(np.int32)
    return np.where(n < 16, n, np.minimum(large, 31))


def _biases(a):
    p, j = np.arange(P)[:, None], np.arange(T)[None, :]
    rel = p - (j - (T - P))
    chunk = a["rel_bias"][0][:, np.clip(rel, -128, 128) + 128]
    chunk = np.where((p < 64) & (j >= T - 64), np.float32(NEG), chunk)
    table = a["rel_bias_2"]
    da = np.where(rel < 0, np.float32(NEG), np.moveaxis(table[_bucket(rel)][..., :4], -1, 0))
    mask = np.where(rel < 0, np.float32(NEG), np.float32(0)).astype(np.float32)
    rel = P + p - np.arange(2 * P)[None, :]
    sw = np.where((rel < 0) | (rel >= 128), np.float32(NEG), np.moveaxis(table[_bucket(rel)][..., 4:], -1, 0))
    return [np.ascontiguousarray(x.astype(np.float32)) for x in (chunk, da, mask, sw)]


def kernel(**inputs):
    import concourse.bacc as bacc
    from concourse.bass_utils import run_bass_kernel_spmd

    a = {k: np.asarray(x) for k, x in inputs.items()}
    tiles = lambda x: np.ascontiguousarray(x.T.reshape(-1, P, T).transpose(1, 0, 2))
    stream = _stream(a)
    ada = np.concatenate([a["ada_w"][0], a["ada_w"][1], a["kv_ada_w"], np.zeros((D, 256), np.float32)], 1)
    ada = np.ascontiguousarray(ada.reshape(KD, P, N_ADA + 1, 256).transpose(2, 1, 0, 3))
    cst = np.zeros((P, 4, P), np.float32)
    cst[:, 0] = np.eye(P)
    cst[:, 1] = 1.0
    cst[:HD, 2, :HD] = 1.0
    cst[HD:, 2, HD:] = 1.0
    for m in range(16):
        cst[ROPE0 + 16 + m, 3, ROPE0 + m] = -1.0
        cst[ROPE0 + m, 3, ROPE0 + 16 + m] = 1.0
    chunk, da, mask, sw = _biases(a)
    ins = dict(w=stream, ada=ada, vec=_vectors(a), cst=cst, x=tiles(a["x"][0]),
               ple=np.stack([tiles(a["p_2"][l, 0]) for l in range(2)]),
               pos=np.ascontiguousarray(np.broadcast_to(a["positions_2"].astype(np.int32), (MLA_QK - ROPE0, T))),
               attn_bias=np.ascontiguousarray(chunk.reshape(KD, 2, P, T).transpose(0, 2, 1, 3)), mask=mask, da_bias=np.ascontiguousarray(da.transpose(1, 0, 2)),
               sw_bias=np.ascontiguousarray(sw.transpose(1, 0, 2)).reshape(P, 4, T))

    counted = {"events": {}, "per_iteration": {}}
    for _ in range(2):
        nc = bacc.Bacc("TRN2", target_bir_lowering=False, num_devices=1)
        io = {k: nc.dram_tensor(f"in_{k}", x.shape, mybir.dt.from_np(x.dtype), kind="ExternalInput").ap()
              for k, x in ins.items()}
        io["out"] = nc.dram_tensor("out", (P, KD, T), F32, kind="ExternalOutput").ap()
        io["units"] = stream.shape[0]
        plan = {"events": {}, "per_iteration": {}, "n": 0}
        build(nc, io, plan, counted)
        counted = plan
    r = run_bass_kernel_spmd(nc, [{f"in_{k}": x for k, x in ins.items()}], core_ids=[0])
    out = r.results[0]["out"]
    return np.ascontiguousarray(out.transpose(1, 0, 2).reshape(D, T).T)[None]
```
